# Optimizing a Trainium2 kernel written in Bass

```python
import math
import jax, jax.numpy as jnp
from jax import lax
import numpy as np

D_MODEL = 2048
BATCH = 1
SEQ = 256
DEPTH = 2

CHUNK = 64
N_MIXERS = 2
N_ATTN_LAYERS = (DEPTH + 1) // 2
N_GLA_LAYERS = DEPTH // 2

DIFF_HEAD_DIM = 128
DIFF_HEADS = D_MODEL // (2 * DIFF_HEAD_DIM)
Q_BLOCK = 128

GLA_HEADS = 4
GLA_KEY_DIM = D_MODEL // 2
GLA_VAL_DIM = D_MODEL
GLA_DK = GLA_KEY_DIM // GLA_HEADS
GLA_DV = GLA_VAL_DIM // GLA_HEADS
GLA_GATE_RANK = 16
GLA_GATE_TAU = 16.0

D_FF = 4 * D_MODEL

DN_ALPHA = (2.0 * DEPTH) ** 0.25
DN_BETA = (8.0 * DEPTH) ** -0.25
LN_EPS = 1e-5
RMS_EPS = 1e-6

kernel_name = "hybrid_diffattn_gla_deepnorm_encoder"

def layer_norm(x, g, b):
    xf = x.astype(jnp.float32)
    mu = jnp.mean(xf, axis=-1, keepdims=True)
    xc = xf - mu
    var = jnp.mean(xc * xc, axis=-1, keepdims=True)
    y = xc * lax.rsqrt(var + LN_EPS) * g.astype(jnp.float32) + b.astype(jnp.float32)
    return y.astype(x.dtype)

def rms_norm(x, g):
    xf = x.astype(jnp.float32)
    y = xf * lax.rsqrt(jnp.mean(xf * xf, axis=-1, keepdims=True) + RMS_EPS) * g.astype(jnp.float32)
    return y.astype(x.dtype)

def diff_attention(x, w_qkv, w_o, lam, subln, lam_init):
    B, S, _ = x.shape
    H, d = DIFF_HEADS, DIFF_HEAD_DIM
    qkv = x @ w_qkv
    q, k, v = jnp.split(qkv, [2 * H * d, 4 * H * d], axis=-1)
    q = q.reshape(B, S, H, 2, d) * (d ** -0.5)
    k = k.reshape(B, S, H, 2, d)
    v = v.reshape(B, S, H, 2 * d)
    lamf = lam.astype(jnp.float32)
    lam_full = (jnp.exp(jnp.sum(lamf[0] * lamf[1])) - jnp.exp(jnp.sum(lamf[2] * lamf[3]))
                + lam_init)
    k_chunk = jnp.arange(S) // CHUNK

    def block(i):
        q_blk = lax.dynamic_slice_in_dim(q, i * Q_BLOCK, Q_BLOCK, axis=1)
        s = jnp.einsum('bqhjd,bkhjd->bhjqk', q_blk, k).astype(jnp.float32)
        q_chunk = (i * Q_BLOCK + jnp.arange(Q_BLOCK)) // CHUNK
        allowed = k_chunk[None, :] <= q_chunk[:, None]
        s = jnp.where(allowed, s, -jnp.inf)
        p = jax.nn.softmax(s, axis=-1)
        w = p[:, :, 0] - lam_full * p[:, :, 1]
        return jnp.einsum('bhqk,bkhe->bqhe', w.astype(v.dtype), v)

    o = lax.map(block, jnp.arange(S // Q_BLOCK))
    o = o.transpose(1, 0, 2, 3, 4).reshape(B, S, H, 2 * d)
    o = rms_norm(o, subln) * (1.0 - lam_init)
    return o.reshape(B, S, H * 2 * d) @ w_o

def gla(x, w_in, w_gk2, b_gk, g_norm, w_o):
    B, S, _ = x.shape
    H, dk, dv = GLA_HEADS, GLA_DK, GLA_DV
    nc = S // CHUNK
    proj = x @ w_in
    q, k, v, r, z = jnp.split(
        proj, [GLA_KEY_DIM, 2 * GLA_KEY_DIM, 2 * GLA_KEY_DIM + GLA_VAL_DIM,
               2 * GLA_KEY_DIM + 2 * GLA_VAL_DIM], axis=-1)
    gk = z @ w_gk2 + b_gk
    log_a = jax.nn.log_sigmoid(gk.astype(jnp.float32)) / GLA_GATE_TAU

    def to_chunks(t, dh):
        return t.astype(jnp.float32).reshape(B, nc, CHUNK, H, dh).transpose(1, 0, 3, 2, 4)

    q = to_chunks(q, dk) * (dk ** -0.5)
    k = to_chunks(k, dk)
    v = to_chunks(v, dv)
    b = jnp.cumsum(to_chunks(log_a, dk), axis=3)
    b_last = b[:, :, :, -1:, :]
    q_dec = q * jnp.exp(b)
    k_inv = k * jnp.exp(-b)
    k_st = k * jnp.exp(b_last - b)

    causal = jnp.tril(jnp.ones((CHUNK, CHUNK), dtype=bool))
    attn = jnp.einsum('nbhtd,nbhsd->nbhts', q_dec, k_inv)
    attn = jnp.where(causal, attn, 0.0)
    o_intra = jnp.einsum('nbhts,nbhsv->nbhtv', attn, v)

    def step(state, inp):
        q_c, k_c, v_c, bl_c = inp
        o_c = jnp.einsum('bhtk,bhkv->bhtv', q_c, state)
        state = (jnp.exp(bl_c)[:, :, 0, :, None] * state
                 + jnp.einsum('bhsk,bhsv->bhkv', k_c, v_c))
        return state, o_c

    state0 = jnp.zeros((B, H, dk, dv), jnp.float32)
    _, o_inter = lax.scan(step, state0, (q_dec, k_st, v, b_last))
    o = (o_intra + o_inter).transpose(1, 0, 3, 2, 4).reshape(B, S, H, dv)
    o = rms_norm(o, g_norm).reshape(B, S, GLA_VAL_DIM) * jax.nn.silu(r.astype(jnp.float32))
    return o.astype(x.dtype) @ w_o

def squared_relu_mlp(x, w1, w2):
    return jnp.square(jax.nn.relu(x @ w1)) @ w2

def setup_inputs(seed: int = 0) -> dict:
    key = jax.random.key(seed)
    ks = jax.random.split(key, 20)
    D = D_MODEL
    NA, NG = N_ATTN_LAYERS, N_GLA_LAYERS

    def nrm(k, shape, scale):
        return jax.random.normal(k, shape, jnp.float32) * scale

    x = nrm(ks[0], (BATCH, SEQ, D), 1.0)

    qk_cols = 4 * DIFF_HEADS * DIFF_HEAD_DIM
    v_cols = 2 * DIFF_HEADS * DIFF_HEAD_DIM
    attn_w_qkv = jnp.concatenate(
        [nrm(ks[1], (NA, D, qk_cols), D ** -0.5),
         nrm(ks[2], (NA, D, v_cols), D ** -0.5 * DN_BETA)], axis=-1)
    attn_w_o = nrm(ks[3], (NA, v_cols, D), v_cols ** -0.5 * DN_BETA)
    attn_lambda = nrm(ks[4], (NA, 4, DIFF_HEAD_DIM), 0.1)
    attn_subln = 1.0 + nrm(ks[5], (NA, 2 * DIFF_HEAD_DIM), 0.01)

    gla_w_in = jnp.concatenate(
        [nrm(ks[6], (NG, D, 2 * GLA_KEY_DIM), D ** -0.5),
         nrm(ks[7], (NG, D, GLA_VAL_DIM), D ** -0.5 * DN_BETA),
         nrm(ks[8], (NG, D, GLA_VAL_DIM), D ** -0.5),
         nrm(ks[9], (NG, D, GLA_GATE_RANK), D ** -0.5)], axis=-1)
    gla_w_gk2 = nrm(ks[10], (NG, GLA_GATE_RANK, GLA_KEY_DIM), GLA_GATE_RANK ** -0.5)
    gla_b_gk = nrm(ks[11], (NG, GLA_KEY_DIM), 0.01)
    gla_norm = 1.0 + nrm(ks[12], (NG, GLA_DV), 0.01)
    gla_w_o = nrm(ks[13], (NG, GLA_VAL_DIM, D), GLA_VAL_DIM ** -0.5 * DN_BETA)

    mlp_w1 = nrm(ks[14], (DEPTH, D, D_FF), D ** -0.5 * DN_BETA)
    mlp_w2 = nrm(ks[15], (DEPTH, D_FF, D), D_FF ** -0.5 * DN_BETA)
    ln_g = 1.0 + nrm(ks[16], (DEPTH, 2, D), 0.01)
    ln_b = nrm(ks[17], (DEPTH, 2, D), 0.01)

    return {"x": x,
            "attn_w_qkv": attn_w_qkv, "attn_w_o": attn_w_o,
            "attn_lambda": attn_lambda, "attn_subln": attn_subln,
            "gla_w_in": gla_w_in, "gla_w_gk2": gla_w_gk2, "gla_b_gk": gla_b_gk,
            "gla_norm": gla_norm, "gla_w_o": gla_w_o,
            "mlp_w1": mlp_w1, "mlp_w2": mlp_w2,
            "ln_g": ln_g, "ln_b": ln_b}

def reference(x, attn_w_qkv, attn_w_o, attn_lambda, attn_subln,
              gla_w_in, gla_w_gk2, gla_b_gk, gla_norm, gla_w_o,
              mlp_w1, mlp_w2, ln_g, ln_b):
    h = x
    for i in range(DEPTH):
        j = i // N_MIXERS
        if i % N_MIXERS == 0:
            lam_init = 0.8 - 0.6 * math.exp(-0.3 * i)
            y = diff_attention(h, attn_w_qkv[j], attn_w_o[j], attn_lambda[j],
                               attn_subln[j], lam_init)
        else:
            y = gla(h, gla_w_in[j], gla_w_gk2[j], gla_b_gk[j], gla_norm[j], gla_w_o[j])
        h = layer_norm(DN_ALPHA * h + y, ln_g[i, 0], ln_b[i, 0])
        f = squared_relu_mlp(h, mlp_w1[i], mlp_w2[i])
        h = layer_norm(DN_ALPHA * h + f, ln_g[i, 1], ln_b[i, 1])
    return h


_drawn_inputs = setup_inputs


def setup_inputs(seed=0):
    import zlib

    import numpy as np

    out = dict(_drawn_inputs(seed))
    spreads = {}
    factors = {'attn_subln': 8.0, 'gla_b_gk': 8.0, 'gla_norm': 8.0, 'ln_g': 2.692, 'ln_b': 2.732}
    for name, (base, spread) in spreads.items():
        noise = np.random.default_rng([zlib.crc32(name.encode()), seed]).standard_normal(out[name].shape)
        drawn = base * np.exp(spread * noise) if base else spread * noise
        out[name] = __import__('jax').numpy.asarray(drawn.astype(out[name].dtype))
    for name, factor in factors.items():
        out[name] = (out[name] * factor).astype(out[name].dtype)
    return out
```

```python
import math
from contextlib import ExitStack

import concourse.bass as bass
from concourse import mybir

F32 = mybir.dt.float32
F32R = mybir.dt.float32r
ALU = mybir.AluOpType
ACT = mybir.ActivationFunctionType
AX_X = mybir.AxisListType.X

P = 128
D = 2048
SEQ = 256
TB = SEQ // P
KT = D // P
COLS = 512
TILES = 4
KPT = KT // TILES
QUARTERS = D // COLS
DEPTH = 2
FF = 4 * D
CHUNKS = FF // D
CHUNK = 64
N_CHUNKS = SEQ // CHUNK

HEADS = 8
DH = 128
PAIRS = HEADS // 2
LAM_INIT = 0.8 - 0.6 * math.exp(-0.3 * 0)
Q_SCALE = DH ** -0.5
MASKED = -3.0e38

GLA_HEADS = 4
KEY = D // 2
DK = KEY // GLA_HEADS
DKT = DK // P
DV = D // GLA_HEADS
RANK = 16
TAU = 16.0
GLA_Q_SCALE = DK ** -0.5

ALPHA = (2.0 * DEPTH) ** 0.25
LN_EPS = 1e-5
RMS_EPS = 1e-6

G_WO = 3 * PAIRS
G_MLP = [G_WO + QUARTERS, 0]
G_GLA = G_MLP[0] + 8 * CHUNKS
G_VR = G_GLA + 4
G_GWO = G_VR + 2 * GLA_HEADS
G_MLP[1] = G_GWO + QUARTERS
N_GROUPS = G_MLP[1] + 8 * CHUNKS
COLS_MLP = [2 * PAIRS, 2 * PAIRS + 4 * CHUNKS + 4]
COLS_GLA = 2 * PAIRS + 4 * CHUNKS
RES_MLP = [QUARTERS, 2 * QUARTERS + 4 * CHUNKS]
RES_GWO = QUARTERS + 4 * CHUNKS
ROWS_WO = PAIRS
ROWS_MLP = [ROWS_WO + QUARTERS, 0]
ROWS_VR = ROWS_MLP[0] + 4 * CHUNKS
ROWS_GWO = ROWS_VR + 2 * GLA_HEADS
ROWS_MLP[1] = ROWS_GWO + QUARTERS
LN_BANKS = (5, 6, 7)


def build(nc, x, attn_w_qkv, attn_w_o, attn_lambda, attn_subln, gla_w_in, gla_w_gk2, gla_b_gk,
          gla_norm, gla_w_o, mlp_w1, mlp_w2, ln_g, ln_b, out):
    ctx = ExitStack()
    with ctx:
        def sb(name, shape, dt=F32):
            return ctx.enter_context(nc.sbuf_tensor(name, shape, dt))

        def sem(name):
            return ctx.enter_context(nc.semaphore(name))

        raw = sb("raw", [P, TILES, KPT, COLS])
        hi = sb("hi", [P, TILES, KPT, COLS], F32R)
        lo = sb("lo", [P, TILES, KPT, COLS], F32R)
        X = sb("X", [P, KT, 2, SEQ], F32R)
        res = sb("res", [P, TB, D])
        f_bytes = KT * 2 * SEQ * 4
        f_at = nc.sbuf_base
        F_hold = sb("F_hold", [P, f_bytes // 4])
        F = nc.alloc_sbuf_tensor_at("F", [P, KT, 2, SEQ], F32R, offset=f_at)
        G = nc.alloc_sbuf_tensor_at("G", [P, GLA_HEADS, DKT, 4, SEQ], F32, offset=f_at)
        G_QD, G_KI, G_D, G_R = range(4)
        wz_hi = sb("wz_hi", [P, KT, RANK], F32R)
        wz_lo = sb("wz_lo", [P, KT, RANK], F32R)
        work = sb("work", [P, 7168])
        ident = sb("ident", [P, P])
        b_gk = sb("b_gk", [P, KEY // P])
        ln_stats = sb("ln_stats", [P, TB, QUARTERS, 6])
        ln_mean_var = sb("ln_mean_var", [P, TB, 2])
        ln_rstd = sb("ln_rstd", [P, TB, 2])
        minus_half = sb("minus_half", [P, 2])
        row_max = sb("row_max", [P, 4])
        neg_max = sb("neg_max", [P, 4])
        row_sum = sb("row_sum", [P, 4])
        inv_sum = sb("inv_sum", [P, 4])
        neg_lam_inv = sb("neg_lam_inv", [P, 2])
        lam_parts = sb("lam_parts", [P, 4])
        neg_lam = sb("neg_lam", [P, 1])
        sq_sum = sb("sq_sum", [P, 2, 2])
        rms_rstd = sb("rms_rstd", [P, 2, 2, 2])
        chunk_decay = sb("chunk_decay", [P, GLA_HEADS * DKT, 2])

        def part(at, *dims):
            n = math.prod(dims)
            v = work[:, at:at + n]
            if len(dims) == 1:
                return v
            names = "abc"[:len(dims)]
            return v.rearrange(f"p ({' '.join(names)}) -> p {' '.join(names)}",
                               **{k: d for k, d in zip(names, dims)})

        ln_gb = part(0, 2, D)
        mlp_half = part(4096, 2, 2, SEQ)
        mlp_hidden = part(5120, 2, 2, SEQ)
        qT = part(0, 4, SEQ)
        kT = part(1024, 4, SEQ)
        v_rows = part(2048, TB, COLS)
        probs = part(3072, 2, 384)
        mixed = part(3840, 384)
        mixedT = part(4224, 2, 384)
        o_norm = part(4992, 2, 2, SEQ)
        mask = part(6016, 384)
        subln = part(6400, 256)
        qk_half = part(6656, 2, SEQ)
        lam_rows = part(4992, 4, DH)
        wz_raw = part(2048, KT, RANK)
        cum = part(0, GLA_HEADS * DKT, SEQ)
        gate = part(2048, GLA_HEADS * DKT, SEQ)
        gk_tmp = part(4096, GLA_HEADS * DKT, SEQ)
        to_last = part(4096, GLA_HEADS * DKT, 3, CHUNK)
        zT = part(4096, SEQ)
        w_gk2 = part(4352, KEY)
        z_half = part(5376, SEQ)
        scan_mask = part(6144, SEQ)
        gla_half = part(2048, 2, 2, SEQ)
        gla_qk = part(3072, 2, 2, SEQ)
        keys = part(0, DKT, 4, SEQ)
        gla_v = part(2048, TB, DV)
        silu_r = part(3072, TB, DV)
        sig = part(4096, DV)
        pairT = part(4608, 384)
        gla_o = part(4992, TB, DV)
        gla_gain = part(6016, DV)

        ps = ctx.enter_context(nc.psum_tensor("ps", [P, 8, COLS], F32))

        x_loaded = [sem(f"x_loaded{t}") for t in range(TB)]
        raw_full = [sem(f"raw_full{j}") for j in range(TILES)]
        small_loaded = sem("small_loaded")
        gb_loaded = sem("gb_loaded")
        gk2_loaded = sem("gk2_loaded")
        gain_loaded = sem("gain_loaded")
        out_stored = sem("out_stored")
        consts_ready = sem("consts_ready")
        hi_ready = sem("hi_ready")
        lo_ready = sem("lo_ready")
        w_used = sem("w_used")
        first_block_done = sem("first_block_done")
        half_copied = sem("half_copied")
        halves_added = sem("halves_added")
        res_added = sem("res_added")
        ln_dve = sem("ln_dve")
        ln_var = sem("ln_var")
        ln_pow = sem("ln_pow")
        ln_quarter = sem("ln_quarter")
        ln_turned = sem("ln_turned")
        x_hi = sem("x_hi")
        x_lo = sem("x_lo")
        res_scaled = sem("res_scaled")
        squared = sem("squared")
        f_hi = sem("f_hi")
        f_lo = sem("f_lo")
        set_up = sem("set_up")
        wz_hi_ready = sem("wz_hi_ready")
        lam_dots = sem("lam_dots")
        lam_exps = sem("lam_exps")
        v_copied = sem("v_copied")
        scores_done = sem("scores_done")
        scores_seen = sem("scores_seen")
        pairs_seen = sem("pairs_seen")
        maxes = sem("maxes")
        neg_max_ready = sem("neg_max_ready")
        exps_done = sem("exps_done")
        mix = sem("mix")
        mixed_ready = sem("mixed_ready")
        mixed_turned = sem("mixed_turned")
        mixedT_ready = sem("mixedT_ready")
        pv_done = sem("pv_done")
        sq_done = sem("sq_done")
        ms_ready = sem("ms_ready")
        rms_pow = sem("rms_pow")
        o_normed = sem("o_normed")
        o_turned = sem("o_turned")
        o_hi = sem("o_hi")
        o_lo = sem("o_lo")
        z_done = sem("z_done")
        z_half_copied = sem("z_half_copied")
        zT_ready = sem("zT_ready")
        gk_done = sem("gk_done")
        gk_act = sem("gk_act")
        gate_ready = sem("gate_ready")
        scanned = sem("scanned")
        to_last_ready = sem("to_last_ready")
        decays_ready = sem("decays_ready")
        q_ready = sem("q_ready")
        key_step = sem("key_step")
        keys_staged = sem("keys_staged")
        pairs_done = sem("pairs_done")
        pairs_copied = sem("pairs_copied")
        pairs_masked = sem("pairs_masked")
        go_done = sem("go_done")
        gsq_done = sem("gsq_done")
        gms_ready = sem("gms_ready")
        grms_pow = sem("grms_pow")
        exp_r = sem("exp_r")
        sig_step = sem("sig_step")
        r_gated = sem("r_gated")
        r_gained = sem("r_gained")
        go_normed = sem("go_normed")
        go_turned = sem("go_turned")
        go_hi = sem("go_hi")
        go_lo = sem("go_lo")

        w_qkv = attn_w_qkv[0].rearrange("(t p) n -> p t n", p=P)
        w_o = attn_w_o[0].rearrange("(t p) n -> p t n", p=P)
        w_in = gla_w_in[0].rearrange("(t p) n -> p t n", p=P)
        w_go = gla_w_o[0].rearrange("(t p) n -> p t n", p=P)
        w_1 = [mlp_w1[m].rearrange("(t p) n -> p t n", p=P) for m in range(DEPTH)]
        w_2 = [mlp_w2[m].rearrange("(t p) n -> p t n", p=P) for m in range(DEPTH)]
        x_rows = x[0].rearrange("(t p) n -> p t n", p=P)
        out_rows = out[0].rearrange("(t p) n -> p t n", p=P)

        def blk(t):
            return slice(t * P, (t + 1) * P)

        block = ctx.enter_context(nc.Block())

        @block.sync
        def _(sp):
            def load_group(g, w, col, row=0):
                for j in range(TILES):
                    if not isinstance(g, int) or g:
                        sp.wait_ge(lo_ready, 4 * g + j - 3)
                    sp.dma_start(raw[:, j], w[:, bass.ds(row + KPT * j, KPT), bass.ds(col, COLS)]
                                 ).then_inc(raw_full[j], 16)

            for t in range(TB):
                sp.dma_start(res[:, t, :], x_rows[:, t, :]).then_inc(x_loaded[t], 16)
            load_group(0, w_qkv, 0)
            load_group(1, w_qkv, D)
            with sp.Fori(0, PAIRS - 1) as c:
                load_group(3 * c + 2, w_qkv, 2 * D + COLS * c)
                load_group(3 * c + 3, w_qkv, COLS * c + COLS)
                load_group(3 * c + 4, w_qkv, COLS * c + (D + COLS))
            load_group(3 * PAIRS - 1, w_qkv, 2 * D + COLS * (PAIRS - 1))
            with sp.Fori(0, QUARTERS) as q:
                load_group(q + G_WO, w_o, COLS * q)

            def load_mlp(m):
                with sp.Fori(0, CHUNKS) as ch:
                    with sp.Fori(0, QUARTERS) as q:
                        load_group(8 * ch + q + G_MLP[m], w_1[m], D * ch + COLS * q)
                    with sp.Fori(0, QUARTERS) as q:
                        load_group(8 * ch + q + (G_MLP[m] + 4), w_2[m], COLS * q, KT * ch)

            load_mlp(0)
            with sp.Fori(0, 4) as q:
                load_group(q + G_GLA, w_in, COLS * q)
            with sp.Fori(0, GLA_HEADS) as h:
                load_group(2 * h + G_VR, w_in, COLS * h + 2 * KEY)
                load_group(2 * h + (G_VR + 1), w_in, COLS * h + (2 * KEY + D))
            with sp.Fori(0, QUARTERS) as q:
                load_group(q + G_GWO, w_go, COLS * q)
            load_mlp(1)
            for t in range(TB):
                sp.wait_ge(ln_quarter, 8 * 3 + 4 * t + 4)
                sp.dma_start(out_rows[:, t, :], res[:, t, :]).then_inc(out_stored, 16)
            sp.wait_ge(out_stored, 16 * TB)

        @block.gpsimd
        def _(pool):
            def load_gb(layer, i):
                for n, src in enumerate((ln_g, ln_b)):
                    pool.dma_start(ln_gb[:, n, :], src[layer, i].partition_broadcast(P)).then_inc(gb_loaded, 16)

            def scale_residual(L):
                for i in range(TB * QUARTERS):
                    t, q = i // QUARTERS, i % QUARTERS
                    pool.wait_ge(ln_turned, 8 * L + i + 1)
                    r = res[:, t, q * COLS:(q + 1) * COLS]
                    pool.tensor_scalar(r, r, ALPHA, None, ALU.mult).then_inc(res_scaled, 1)

            def ln_powers(L):
                for t in range(TB):
                    pool.wait_ge(ln_var, 2 * (L - 1) + t + 1)
                    pool.tensor_tensor(ln_rstd[:, t, 1:2], ln_rstd[:, t, 0:1], minus_half[:, 0:1],
                                       ALU.pow).then_inc(ln_pow, 1)

            def rms_power(n, hp):
                pool.wait_ge(ms_ready, n + 1)
                pool.tensor_tensor(rms_rstd[:, hp, 1, :], rms_rstd[:, hp, 0, :], minus_half[:, :],
                                   ALU.pow).then_inc(rms_pow, 1)

            def gla_power(h):
                pool.wait_ge(gms_ready, h + 1)
                pool.tensor_tensor(rms_rstd[:, 0, 1, :], rms_rstd[:, 0, 0, :], minus_half[:, :],
                                   ALU.pow).then_inc(grms_pow, 1)

            pool.dma_start(lam_rows.rearrange("p a b -> p (a b)"),
                           attn_lambda[0].rearrange("a b -> (a b)").partition_broadcast(P)).then_inc(small_loaded, 16)
            pool.dma_start(subln, attn_subln[0].partition_broadcast(P)).then_inc(small_loaded, 16)
            with nc.allow_non_contiguous_dma(reason="b_gk with a feature on each partition: 4 KB"):
                pool.dma_start(b_gk[:, :], gla_b_gk[0].rearrange("(t p) -> p t", p=P)).then_inc(small_loaded, 16)
            pool.dma_start(wz_raw, w_in[:, :, 2 * KEY + 2 * D:]).then_inc(small_loaded, 16)
            pool.memset(ident[:, :], 0.0).then_inc(consts_ready, 1)
            pool.memset(mask, 0.0).then_inc(consts_ready, 1)
            pool.memset(minus_half[:, :], -0.5).then_inc(consts_ready, 1)
            pool.wait_ge(consts_ready, 3)
            pool.affine_select(out=ident[:, :], in_=ident[:, :], compare_op=ALU.not_equal, fill=1.0, base=0,
                               pattern=[[-1, P]], channel_multiplier=1).then_inc(consts_ready, 1)
            pool.memset(mask[0:CHUNK, CHUNK:P], MASKED).then_inc(consts_ready, 1)
            pool.memset(mask[0:CHUNK, 384 - CHUNK:384], MASKED).then_inc(consts_ready, 1)
            scale_residual(0)
            with pool.Fori(0, PAIRS) as c:
                rms_power(2 * c, 0)
                rms_power(2 * c + 1, 1)
            pool.wait_ge(o_turned, HEADS)
            load_gb(0, 0)
            ln_powers(1)
            scale_residual(1)
            pool.wait_ge(ln_quarter, 8)
            load_gb(0, 1)
            ln_powers(2)
            scale_residual(2)
            pool.wait_ge(ln_quarter, 16)
            pool.dma_start(w_gk2[0:RANK, :], gla_w_gk2[0]).then_inc(gk2_loaded, 16)
            sm = scan_mask.rearrange("p (c t) -> p c t", t=CHUNK)
            pool.memset(scan_mask, 1.0).then_inc(consts_ready, 1)
            pool.wait_ge(consts_ready, 7)
            pool.memset(sm[:, :, 0:1], 0.0).then_inc(consts_ready, 1)

            def stage_keys(h):
                if not isinstance(h, int) or h:
                    pool.wait_ge(pairs_done, h)
                pool.tensor_copy(part(0, 2048), G[:, bass.ds(h, 1)].rearrange("p h a b c -> p (h a b c)")
                                 ).then_inc(keys_staged, 1)

            def mask_pairs(h):
                pool.wait_ge(pairs_copied, h + 1)
                pool.sem_inc(pairs_seen, 1)
                d = pairT.rearrange("p (b t) -> p b t", t=P)[:, 0::2, :]
                pool.affine_select(out=d, in_=d, compare_op=ALU.is_ge, fill=0.0, base=0,
                                   pattern=[[0, 2], [1, P]], channel_multiplier=-1).then_inc(pairs_masked, 1)

            def gain_r(h):
                for t in range(TB):
                    pool.wait_ge(r_gated, 2 * h + t + 1)
                    pool.tensor_tensor(silu_r[:, t, :], silu_r[:, t, :], gla_gain, ALU.mult).then_inc(r_gained, 1)

            pool.wait_ge(key_step, 8 * GLA_HEADS)
            stage_keys(0)
            pool.dma_start(gla_gain, gla_norm[0].partition_broadcast(P)).then_inc(gain_loaded, 16)
            pool.wait_ge(gain_loaded, 16)
            with pool.Fori(0, GLA_HEADS - 1) as h:
                mask_pairs(h)
                stage_keys(h + 1)
                gla_power(h)
                gain_r(h)
            mask_pairs(GLA_HEADS - 1)
            gla_power(GLA_HEADS - 1)
            gain_r(GLA_HEADS - 1)
            pool.wait_ge(go_turned, 2 * GLA_HEADS)
            load_gb(1, 0)
            ln_powers(3)
            scale_residual(3)
            pool.wait_ge(ln_quarter, 24)
            load_gb(1, 1)
            ln_powers(4)

        @block.tensor
        def _(pe):
            def mm(o, w, m, start, stop):
                return pe.matmul(o, w, m, start=start, stop=stop)

            def rows_pass(g, t, acts, after=None, ready=None):
                acc = ps[:, 4 * t, :]
                for j in range(TILES):
                    if t == 0:
                        pe.wait_ge(lo_ready, 4 * g + j + 1)
                        if ready:
                            pe.wait_ge(*ready(j))
                    for k in range(KPT):
                        a = 4 * j + k
                        first, last = a == 0, a == KT - 1
                        mm(acc, acts[:, a, 0, blk(t)], hi[:, j, k, :], first, False)
                        mm(acc, acts[:, a, 0, blk(t)], lo[:, j, k, :], False, False)
                        m = mm(acc, acts[:, a, 1, blk(t)], hi[:, j, k, :], False, last)
                    if t == 1:
                        m.then_inc(w_used, 1)
                    elif j == TILES - 1:
                        m.then_inc(first_block_done, 1)
                    if after and (t, j) in after:
                        after[t, j]()

            def cols_group(g, par, acts, after=None, ready=None):
                for j in range(TILES):
                    pe.wait_ge(lo_ready, 4 * g + j + 1)
                    if ready:
                        pe.wait_ge(*ready(j))
                    for k in range(KPT):
                        a = 4 * j + k
                        first, last = a == 0, a == KT - 1
                        for i in range(4):
                            acc = ps[:, 4 * par + i, :]
                            if first:
                                mm(acc, hi[:, j, k, blk(i)], acts[:, a, :, :], True, False)
                            m = mm(acc[:, 0:SEQ], lo[:, j, k, blk(i)], acts[:, a, 0, :], False, False)
                            if not first:
                                m = mm(acc, hi[:, j, k, blk(i)], acts[:, a, :, :], False, last)
                    m.then_inc(w_used, 1)
                    if after and j in after:
                        after[j]()

            def turn_quarter(L, i):
                t, q = i // QUARTERS, i % QUARTERS
                if L:
                    pe.wait_ge(ln_quarter, 8 * (L - 1) + i + 1)
                if i >= len(LN_BANKS):
                    pe.wait_ge(x_lo, 8 * L + i + 1 - len(LN_BANKS))
                for b in range(QUARTERS):
                    m = pe.transpose(ps[:, LN_BANKS[i % 3], blk(b)], res[:, t, blk(4 * q + b)], ident[:, :])
                m.then_inc(ln_turned, 1)

            pe.wait_ge(consts_ready, 4)
            for i in range(TB * QUARTERS):
                if i % QUARTERS == 0:
                    pe.wait_ge(x_loaded[i // QUARTERS], 16)
                turn_quarter(0, i)

            def scores(n, hp, c):
                pe.wait_ge(halves_added, 4 * c + 4)
                if hp:
                    pe.wait_ge(maxes, 4 * n)
                for s in range(2):
                    i = 2 * hp + s
                    mm(ps[:, 1 + s, 0:P], qT[:, i, blk(0)], kT[:, i, blk(0)], True, True)
                    m = mm(ps[:, 1 + s, P:P + SEQ], qT[:, i, blk(1)], kT[:, i, :], True, True)
                m.then_inc(scores_done, 1)

            def turn_mixed(n, hp):
                pe.wait_ge(mixed_ready, n + 1)
                for b in range(3):
                    m = pe.transpose(ps[:, 3 + 4 * hp, blk(b)], mixed[:, blk(b)], ident[:, :])
                m.then_inc(mixed_turned, 1)

            def weigh_values(n, hp, c):
                pe.wait_ge(mixedT_ready, n + 1)
                pe.wait_ge(v_copied, 2 * c + 2)
                o, col = ps[:, 5 + hp, :], slice(hp * SEQ, (hp + 1) * SEQ)
                mm(o[:, 0:SEQ], mixedT[:, hp, blk(0)], v_rows[:, 0, col], True, True)
                mm(o[:, SEQ:], mixedT[:, hp, blk(1)], v_rows[:, 0, col], True, False)
                mm(o[:, SEQ:], mixedT[:, hp, blk(2)], v_rows[:, 1, col], False, True).then_inc(pv_done, 1)

            def turn_output(n, hp):
                pe.wait_ge(o_normed, 2 * n + 2)
                if hp == 0:
                    pe.wait_ge(mixedT_ready, n + 2)
                bank = ps[:, 7 - 2 * hp, :]
                for e in range(2):
                    for t in range(TB):
                        m = pe.transpose(bank[:, e * SEQ + t * P:e * SEQ + (t + 1) * P],
                                         o_norm[:, hp, t, blk(e)], ident[:, :])
                m.then_inc(o_turned, 1)

            def v_group(g, c):
                pe.wait_ge(halves_added, 4 * c + 2)
                rows_pass(g, 0, X, {(0, 1): lambda: scores(2 * c, 0, c)})
                pe.wait_ge(halves_added, 4 * c + 4)
                rows_pass(g, 1, X, {(1, 0): lambda: scores(2 * c + 1, 1, c), (1, 1): lambda: turn_mixed(2 * c, 0)})

            cols_group(0, 0, X, ready=lambda j: (x_lo, 4 + j + 1))
            pe.wait_ge(x_lo, 8)
            cols_group(1, 1, X)
            with pe.Fori(0, PAIRS - 1) as c:
                v_group(3 * c + 2, c)
                pe.wait_ge(v_copied, 2 * c + 1)
                pe.wait_ge(maxes, 8 * c + 8)
                pe.wait_ge(mixedT_ready, 2 * c + 1)
                cols_group(3 * c + 3, 0, X, {
                    0: lambda: (weigh_values(2 * c, 0, c), turn_mixed(2 * c + 1, 1)),
                    1: lambda: weigh_values(2 * c + 1, 1, c),
                    2: lambda: (turn_output(2 * c, 0), turn_output(2 * c + 1, 1))})
                pe.wait_ge(v_copied, 2 * c + 2)
                pe.wait_ge(o_lo, 2 * c + 2)
                cols_group(3 * c + 4, 1, X)
            c = PAIRS - 1
            v_group(3 * c + 2, c)
            pe.wait_ge(v_copied, 2 * c + 1)
            rows_pass(G_WO, 0, F, {
                (0, 0): lambda: (weigh_values(2 * c, 0, c), turn_mixed(2 * c + 1, 1)),
                (0, 1): lambda: weigh_values(2 * c + 1, 1, c),
                (0, 2): lambda: (turn_output(2 * c, 0), turn_output(2 * c + 1, 1))},
                ready=lambda j: (o_lo, 2 * j + 2))
            pe.wait_ge(v_copied, 2 * c + 2)
            rows_pass(G_WO, 1, F)

            def out_groups(g0, r0, n, acts):
                with pe.Fori(0, n) as q:
                    pe.wait_ge(res_added, 2 * q + (2 * r0 - 1))
                    rows_pass(q + g0, 0, acts)
                    pe.wait_ge(res_added, 2 * q + 2 * r0)
                    rows_pass(q + g0, 1, acts)

            def last_out_group(g, r, acts, L):
                pe.wait_ge(res_added, 2 * r - 1)
                rows_pass(g, 0, acts)
                pe.wait_ge(res_added, 2 * r)
                if L == 4:
                    rows_pass(g, 1, acts)
                    return
                rows_pass(g, 1, acts, {(1, 1): lambda: turn_quarter(L, 0),
                                       (1, 2): lambda: (turn_quarter(L, 1), turn_quarter(L, 2)),
                                       (1, 3): lambda: turn_quarter(L, 3)})
                for i in range(QUARTERS, TB * QUARTERS):
                    turn_quarter(L, i)

            out_groups(G_WO + 1, 1, QUARTERS - 2, F)
            last_out_group(G_WO + 3, 3, F, 1)

            def up_pair(m, L, g, n, r, first):
                pe.wait_ge(res_added, 2 * r - 1)
                pe.wait_ge(halves_added, 2 * n - 2)
                cols_group(g, 0, X, ready=(lambda j: (x_lo, 8 * L + 4 + j + 1)) if first else None)
                pe.wait_ge(res_added, 2 * r)
                pe.wait_ge(halves_added, 2 * n)
                cols_group(g + 1, 1, X)

            def down_first(m, ch, g, n, r):
                pe.wait_ge(halves_added, 2 * n - 2)
                rows_pass(g, 0, F, ready=lambda j: (f_lo, 8 * ch + (32 * m + 2 * j + 2)))
                pe.wait_ge(halves_added, 2 * n)
                rows_pass(g, 1, F)

            def mlp(m, L):
                g0, n0, r0 = G_MLP[m], COLS_MLP[m], RES_MLP[m]
                up_pair(m, L, g0, n0, r0, True)
                up_pair(m, L, g0 + 2, n0 + 2, r0, False)
                down_first(m, 0, g0 + 4, n0 + 4, r0)
                out_groups(g0 + 5, r0 + 1, 3, F)
                with pe.Fori(1, CHUNKS - 1) as ch:
                    with pe.Fori(0, 2) as p:
                        up_pair(m, L, 8 * ch + 2 * p + g0, 4 * ch + 2 * p + n0, 4 * ch + r0, False)
                    down_first(m, ch, 8 * ch + (g0 + 4), 4 * ch + (n0 + 4), 4 * ch + r0)
                    with pe.Fori(0, 3) as q:
                        pe.wait_ge(res_added, 8 * ch + 2 * q + (2 * r0 + 1))
                        rows_pass(8 * ch + q + (g0 + 5), 0, F)
                        pe.wait_ge(res_added, 8 * ch + 2 * q + (2 * r0 + 2))
                        rows_pass(8 * ch + q + (g0 + 5), 1, F)
                ch = CHUNKS - 1
                with pe.Fori(0, 2) as p:
                    up_pair(m, L, 2 * p + (g0 + 8 * ch), 2 * p + (n0 + 4 * ch), r0 + 4 * ch, False)
                down_first(m, ch, g0 + 8 * ch + 4, n0 + 4 * ch + 4, r0 + 4 * ch)
                out_groups(g0 + 8 * ch + 5, r0 + 4 * ch + 1, 2, F)
                last_out_group(g0 + 8 * ch + 7, r0 + 4 * ch + 3, F, L + 1)

            mlp(0, 1)

            for a in range(KT):
                if a % KPT == 0:
                    pe.wait_ge(x_lo, 16 + 4 + a // KPT + 1)
                z = ps[0:RANK, 4, :]
                if a == 0:
                    mm(z, wz_hi[:, a, :], X[:, a, :, :], True, False)
                m = mm(z[:, 0:SEQ], wz_lo[:, a, :], X[:, a, 0, :], False, False)
                if a:
                    m = mm(z, wz_hi[:, a, :], X[:, a, :, :], False, a == KT - 1)
            m.then_inc(z_done, 1)

            def gate_scores():
                pe.wait_ge(zT_ready, 1)
                pe.wait_ge(gk2_loaded, 16)
                for i in range(KEY // P):
                    m = mm(ps[:, 4 + i // 2, (i % 2) * SEQ:(i % 2 + 1) * SEQ], w_gk2[0:RANK, blk(i)],
                           zT[0:RANK, :], True, True)
                m.then_inc(gk_done, 1)

            pe.wait_ge(res_added, 2 * RES_GWO)
            cols_group(G_GLA, 0, X, {0: gate_scores})
            pe.wait_ge(gk_act, 1)
            cols_group(G_GLA + 1, 1, X)
            pe.wait_ge(halves_added, 2 * COLS_GLA + 2)
            cols_group(G_GLA + 2, 0, X)
            pe.wait_ge(halves_added, 2 * COLS_GLA + 4)
            cols_group(G_GLA + 3, 1, X)

            def key_pairs(h):
                pe.wait_ge(keys_staged, h + 1)
                plan = [(0, 0, G_KI, 0), (1, 0, G_D, 0), (2, 0, G_R, 0), (2, 1, G_KI, P), (3, 0, G_R, P), (3, 1, G_D, P)]
                for chunk, sblk, kind, at in plan:
                    col = chunk * CHUNK if sblk == 0 else SEQ + (chunk - 2) * CHUNK
                    for e in range(DKT):
                        m = mm(ps[:, 1, col:col + CHUNK], keys[:, e, kind, at:at + P],
                               keys[:, e, G_QD, chunk * CHUNK:(chunk + 1) * CHUNK], e == 0, e == DKT - 1)
                m.then_inc(pairs_done, 1)

            def weigh_gla(h):
                pe.wait_ge(pairs_masked, h + 1)
                pe.wait_ge(v_copied, 2 * h + (2 * PAIRS + 2))
                mm(ps[:, 2, :], pairT[:, 0:P], gla_v[:, 0, :], True, True)
                mm(ps[:, 3, :], pairT[:, P:2 * P], gla_v[:, 0, :], True, False)
                mm(ps[:, 3, :], pairT[:, 2 * P:3 * P], gla_v[:, 1, :], False, True).then_inc(go_done, 1)

            def turn_gla(h, t):
                pe.wait_ge(go_normed, 2 * h + t + 1)
                for e in range(DV // P):
                    m = pe.transpose(ps[:, 5 + t, blk(e)], gla_o[:, t, blk(e)], ident[:, :])
                m.then_inc(go_turned, 1)

            def r_group(h):
                pe.wait_ge(v_copied, 2 * h + (2 * PAIRS + 1))
                rows_pass(2 * h + (G_VR + 1), 0, X, {(0, 0): lambda: key_pairs(h), (0, 3): lambda: weigh_gla(h)})
                pe.wait_ge(v_copied, 2 * h + (2 * PAIRS + 2))
                rows_pass(2 * h + (G_VR + 1), 1, X)

            pe.wait_ge(halves_added, 2 * COLS_GLA + 6)
            rows_pass(G_VR, 0, X)
            pe.wait_ge(halves_added, 2 * COLS_GLA + 8)
            rows_pass(G_VR, 1, X)
            with pe.Fori(0, GLA_HEADS - 1) as h:
                r_group(h)
                pe.wait_ge(r_gated, 2 * h + 1)
                rows_pass(2 * h + (G_VR + 2), 0, X, {(0, 1): lambda: turn_gla(h, 0), (0, 2): lambda: turn_gla(h, 1)})
                pe.wait_ge(r_gated, 2 * h + 2)
                rows_pass(2 * h + (G_VR + 2), 1, X)
            h = GLA_HEADS - 1
            r_group(h)
            pe.wait_ge(r_gated, 2 * h + 1)
            rows_pass(G_GWO, 0, F, {(0, 1): lambda: turn_gla(h, 0), (0, 2): lambda: turn_gla(h, 1)},
                      ready=lambda j: (go_lo, 2 * j + 2))
            pe.wait_ge(r_gated, 2 * h + 2)
            rows_pass(G_GWO, 1, F)
            out_groups(G_GWO + 1, RES_GWO + 1, QUARTERS - 2, F)
            last_out_group(G_GWO + 3, RES_GWO + 3, F, 3)
            mlp(1, 3)

        @block.scalar
        def _(act):
            def split_hi(g, j):
                act.wait_ge(raw_full[j], 16 * g + 16)
                if not isinstance(g, int) or g:
                    act.wait_ge(w_used, 4 * g + j - 3)
                act.activation(hi[:, j], raw[:, j], ACT.Copy).then_inc(hi_ready, 1)

            def split_all(g):
                for j in range(TILES):
                    split_hi(g, j)

            def copy_halves(g, n, par, dst, slots=2, scale=1.0):
                act.wait_ge(w_used, 4 * g + 4)
                for s in range(2):
                    if slots == 1:
                        if s or not isinstance(n, int) or n:
                            act.wait_ge(halves_added, 2 * n + s)
                    elif not isinstance(n, int) or n:
                        act.wait_ge(halves_added, 2 * n + s - 1)
                    b = 4 * par + 2 * s
                    d = dst if slots == 1 else dst[:, s]
                    act.activation(d, ps[:, b:b + 2, SEQ:], ACT.Copy, scale=scale).then_inc(half_copied, 1)

            def x_hi_quarter(L, i):
                t, q = i // QUARTERS, i % QUARTERS
                act.wait_ge(ln_turned, 8 * L + i + 1)
                act.activation(X[:, 4 * q:4 * q + 4, 0, blk(t)],
                               ps[:, LN_BANKS[i % 3], :].rearrange("p (b t) -> p b t", t=P),
                               ACT.Copy).then_inc(x_hi, 1)

            act.wait_ge(small_loaded, 64)
            act.activation(wz_hi[:, :, :], wz_raw, ACT.Copy).then_inc(wz_hi_ready, 1)
            act.wait_ge(lam_dots, 2)
            act.activation(lam_parts[:, 2:4], lam_parts[:, 0:2], ACT.Exp).then_inc(lam_exps, 1)
            for i in range(TB * QUARTERS):
                x_hi_quarter(0, i)
                if i % 2:
                    split_hi(0, i // 2)

            def exps(n, hp):
                act.wait_ge(neg_max_ready, n + 1)
                for s in range(2):
                    for t, (a, b) in enumerate(((0, P), (P, 384))):
                        i = 2 * s + t
                        act.activation(probs[:, s, a:b], probs[:, s, a:b], ACT.Exp, bias=neg_max[:, i:i + 1],
                                       accum_out=row_sum[:, i:i + 1]).then_inc(exps_done, 1)

            def copy_mixedT(n, hp):
                act.wait_ge(mixed_turned, n + 1)
                act.activation(mixedT[:, hp, :], ps[:, 3 + 4 * hp, 0:384], ACT.Copy).then_inc(mixedT_ready, 1)

            def squares(n, hp):
                act.wait_ge(pv_done, n + 1)
                for t in range(TB):
                    act.activation(o_norm[:, hp, t, :], ps[:, 5 + hp, t * SEQ:(t + 1) * SEQ], ACT.Square,
                                   accum_out=sq_sum[:, hp, t:t + 1]).then_inc(sq_done, 1)

            def o_hi_head(n, hp):
                act.wait_ge(o_turned, n + 1)
                act.activation(F[:, bass.ds(2 * n, 2), 0, :],
                               ps[:, 7 - 2 * hp, :].rearrange("p (e t) -> p e t", e=2), ACT.Copy).then_inc(o_hi, 1)

            def copy_v(k, bank_done, dst):
                act.wait_ge(*bank_done)
                act.activation(dst, ps[:, 4 * k, :], ACT.Copy).then_inc(v_copied, 1)

            def v_window(g, c):
                exps(2 * c, 0)
                copy_v(0, (first_block_done, c + 1), v_rows[:, 0, :])
                split_hi(g + 1, 0)
                exps(2 * c + 1, 1)
                split_hi(g + 1, 1)
                copy_mixedT(2 * c, 0)
                split_hi(g + 1, 2)
                split_hi(g + 1, 3)
                copy_v(1, (w_used, 4 * g + 4), v_rows[:, 1, :])

            split_all(1)
            copy_halves(0, 0, 0, qk_half, 1, Q_SCALE)
            split_all(2)
            copy_halves(1, 1, 1, qk_half, 1)
            with act.Fori(0, PAIRS - 1) as c:
                v_window(3 * c + 2, c)
                g = 3 * c + 3
                split_hi(g + 1, 0)
                copy_mixedT(2 * c + 1, 1)
                squares(2 * c, 0)
                split_hi(g + 1, 1)
                squares(2 * c + 1, 1)
                split_hi(g + 1, 2)
                o_hi_head(2 * c, 0)
                o_hi_head(2 * c + 1, 1)
                split_hi(g + 1, 3)
                copy_halves(g, 2 * c + 2, 0, qk_half, 1, Q_SCALE)
                split_all(g + 2)
                copy_halves(g + 1, 2 * c + 3, 1, qk_half, 1)
            c = PAIRS - 1
            v_window(3 * c + 2, c)
            copy_mixedT(2 * c + 1, 1)
            squares(2 * c, 0)
            squares(2 * c + 1, 1)
            o_hi_head(2 * c, 0)
            o_hi_head(2 * c + 1, 1)
            split_all(G_WO + 1)
            with act.Fori(0, 2) as q:
                split_all(q + (G_WO + 2))

            def ln_window(g, L):
                if L == 4:
                    return
                split_hi(g + 1, 0)
                x_hi_quarter(L, 0)
                split_hi(g + 1, 1)
                x_hi_quarter(L, 1)
                x_hi_quarter(L, 2)
                split_hi(g + 1, 2)
                for i in range(QUARTERS - 1, TB * QUARTERS):
                    x_hi_quarter(L, i)
                split_hi(g + 1, 3)

            ln_window(G_WO + 3, 1)

            def up_window(g, n, par, k, fk):
                split_all(g + 1)
                copy_halves(g, n, par, mlp_half)
                for s in range(2):
                    act.wait_ge(squared, k + (s + 1))
                    act.activation(F[:, bass.ds(fk + 2 * s, 2), 0, :], mlp_hidden[:, s], ACT.Copy).then_inc(f_hi, 1)

            def mlp(m, L):
                g0, n0 = G_MLP[m], COLS_MLP[m]
                with act.Fori(0, CHUNKS - 1) as ch:
                    with act.Fori(0, 2) as p:
                        for e in range(2):
                            up_window(8 * ch + 2 * p + (g0 + e), 4 * ch + 2 * p + (n0 + e), e,
                                      8 * ch + 4 * p + (32 * m + 2 * e), 8 * p + 4 * e)
                    with act.Fori(0, 4) as q:
                        split_all(8 * ch + q + (g0 + 5))
                ch = CHUNKS - 1
                with act.Fori(0, 2) as p:
                    for e in range(2):
                        up_window(2 * p + (g0 + e + 8 * ch), 2 * p + (n0 + e + 4 * ch), e,
                                  4 * p + (32 * m + 2 * e + 8 * ch), 8 * p + 4 * e)
                with act.Fori(0, 3) as q:
                    split_all(q + (g0 + 8 * ch + 5))
                ln_window(g0 + 8 * ch + 7, L + 1)

            mlp(0, 1)

            act.wait_ge(z_done, 1)
            act.activation(z_half[0:RANK, :], ps[0:RANK, 4, SEQ:], ACT.Copy).then_inc(z_half_copied, 1)
            split_hi(G_GLA + 1, 0)
            act.wait_ge(gk_done, 1)
            for i in range(KEY // P):
                a = act.activation(gate[:, i, :], ps[:, 4 + i // 2, (i % 2) * SEQ:(i % 2 + 1) * SEQ],
                                   ACT.Identity, bias=b_gk[:, i:i + 1])
            a.then_inc(gk_act, 1)
            act.wait_ge(gk_act, 1)
            act.activation(gk_tmp, gate, ACT.Abs).then_inc(gk_act, 1)
            act.wait_ge(gk_act, 2)
            act.activation(gk_tmp, gk_tmp, ACT.Exp, scale=-1.0).then_inc(gk_act, 1)
            act.wait_ge(gk_act, 3)
            act.activation(gk_tmp, gk_tmp, ACT.Ln, bias=1.0).then_inc(gk_act, 1)
            for j in range(1, TILES):
                split_hi(G_GLA + 1, j)
            act.wait_ge(scanned, 8)
            Gf = G[:, :, :, :, :].rearrange("p h e k t -> p (h e) k t")
            act.activation(Gf[:, :, G_QD, :], cum, ACT.Exp, scale=1.0 / TAU).then_inc(decays_ready, 1)
            copy_halves(G_GLA, COLS_GLA, 0, gla_half)
            act.activation(Gf[:, :, G_KI, :], cum, ACT.Exp, scale=-1.0 / TAU).then_inc(decays_ready, 1)
            act.wait_ge(to_last_ready, 1)
            act.activation(Gf[:, :, G_D, :].rearrange("p i (b c t) -> p i b c t", b=2, c=2)[:, :, :, 0, :],
                           to_last[:, :, 0::2, :], ACT.Exp, scale=1.0 / TAU).then_inc(decays_ready, 1)
            act.activation(Gf[:, :, G_R, CHUNK:P], to_last[:, :, 1, :], ACT.Exp, scale=1.0 / TAU
                           ).then_inc(decays_ready, 1)
            act.activation(chunk_decay[:, :, :],
                           cum.rearrange("p i (c t) -> p i c t", t=CHUNK)[:, :, 1:3, CHUNK - 1],
                           ACT.Exp, scale=1.0 / TAU).then_inc(decays_ready, 1)
            split_all(G_GLA + 2)
            copy_halves(G_GLA + 1, COLS_GLA + 1, 1, gla_half)
            split_all(G_GLA + 3)
            copy_halves(G_GLA + 2, COLS_GLA + 2, 0, gla_half)
            split_all(G_GLA + 4)
            copy_halves(G_GLA + 3, COLS_GLA + 3, 1, gla_half)

            def o_hi_gla(h, t):
                act.wait_ge(go_turned, 2 * h + t + 1)
                act.activation(F[:, bass.ds(4 * h, 4), 0, blk(t)],
                               ps[:, 5 + t, :].rearrange("p (e t) -> p e t", t=P), ACT.Copy).then_inc(go_hi, 1)

            def exp_r_block(h, t):
                act.wait_ge(*((first_block_done, 2 * h + (ROWS_VR + 2)) if t == 0
                              else (w_used, 8 * h + 4 * (G_VR + 2))))
                if t:
                    act.wait_ge(r_gated, 2 * h + t)
                act.activation(sig, ps[:, 4 * t, :], ACT.Exp, scale=-1.0).then_inc(exp_r, 1)

            def r_window(h):
                act.wait_ge(pairs_done, h + 1)
                act.activation(pairT, ps[:, 1, 0:384], ACT.Copy).then_inc(pairs_copied, 1)
                exp_r_block(h, 0)
                split_hi(2 * h + (G_VR + 2), 0)
                act.wait_ge(go_done, h + 1)
                for t in range(TB):
                    act.activation(gla_o[:, t, :], ps[:, 2 + t, :], ACT.Square,
                                   accum_out=sq_sum[:, 0, t:t + 1]).then_inc(gsq_done, 1)
                for j in range(1, TILES):
                    split_hi(2 * h + (G_VR + 2), j)
                exp_r_block(h, 1)

            act.wait_ge(key_step, 8 * GLA_HEADS)
            copy_v(0, (first_block_done, ROWS_VR + 1), gla_v[:, 0, :])
            split_all(G_VR + 1)
            copy_v(1, (w_used, 4 * G_VR + 4), gla_v[:, 1, :])
            with act.Fori(0, GLA_HEADS - 1) as h:
                r_window(h)
                o_hi_gla(h, 0)
                o_hi_gla(h, 1)
                copy_v(0, (first_block_done, 2 * h + (ROWS_VR + 3)), gla_v[:, 0, :])
                split_all(2 * h + (G_VR + 3))
                copy_v(1, (w_used, 8 * h + 4 * (G_VR + 3)), gla_v[:, 1, :])
            h = GLA_HEADS - 1
            r_window(h)
            o_hi_gla(h, 0)
            o_hi_gla(h, 1)
            split_all(G_GWO + 1)
            with act.Fori(0, 2) as q:
                split_all(q + (G_GWO + 2))
            ln_window(G_GWO + 3, 3)
            mlp(1, 3)

        @block.vector
        def _(dve):
            def split_lo(g, j):
                dve.wait_ge(hi_ready, 4 * g + j + 1)
                dve.tensor_tensor(lo[:, j], raw[:, j], hi[:, j].bitcast(F32), ALU.subtract).then_inc(lo_ready, 1)

            def split_all(g):
                for j in range(TILES):
                    split_lo(g, j)

            def x_lo_quarter(L, i):
                t, q = i // QUARTERS, i % QUARTERS
                dve.wait_ge(x_hi, 8 * L + i + 1)
                dve.tensor_tensor(X[:, 4 * q:4 * q + 4, 1, blk(t)],
                                  ps[:, LN_BANKS[i % 3], :].rearrange("p (b t) -> p b t", t=P),
                                  X[:, 4 * q:4 * q + 4, 0, blk(t)].bitcast(F32), ALU.subtract).then_inc(x_lo, 1)

            def add_residual(t, col, done):
                dve.wait_ge(*done)
                d = res[:, t, bass.ds(col, COLS)]
                dve.tensor_tensor(d, d, ps[:, 4 * t, :], ALU.add).then_inc(res_added, 1)

            dve.wait_ge(consts_ready, 6)
            dve.wait_ge(small_loaded, 64)
            for i in range(2):
                dve.tensor_tensor_reduce(lam_rows[:, 2 * i, :], lam_rows[:, 2 * i, :], lam_rows[:, 2 * i + 1, :],
                                         1.0, 0.0, ALU.mult, ALU.add, lam_parts[:, i:i + 1]).then_inc(lam_dots, 1)
            dve.wait_ge(wz_hi_ready, 1)
            dve.tensor_tensor(wz_lo[:, :, :], wz_raw, wz_hi[:, :, :].bitcast(F32), ALU.subtract).then_inc(set_up, 1)
            dve.tensor_scalar(subln, subln, 1.0 - LAM_INIT, None, ALU.mult).then_inc(set_up, 1)
            dve.wait_ge(lam_exps, 1)
            dve.tensor_scalar(neg_lam[:, :], lam_parts[:, 3:4], lam_parts[:, 2:3], LAM_INIT,
                              ALU.subtract, ALU.subtract).then_inc(set_up, 1)
            for i in range(TB * QUARTERS):
                x_lo_quarter(0, i)
                if i % 2:
                    split_lo(0, i // 2)

            def softmax_max(n, hp):
                if hp:
                    dve.wait_ge(mixed_ready, n)
                dve.wait_ge(scores_done, n + 1)
                dve.sem_inc(scores_seen, 1)
                for s in range(2):
                    for t, (a, b) in enumerate(((0, P), (P, 384))):
                        i = 2 * s + t
                        dve.tensor_tensor_reduce(probs[:, s, a:b], ps[:, 1 + s, a:b], mask[:, a:b], 1.0, MASKED,
                                                 ALU.add, ALU.max, row_max[:, i:i + 1]).then_inc(maxes, 1)
                dve.wait_ge(maxes, 4 * n + 4)
                dve.tensor_scalar(neg_max[:, :], row_max[:, :], -1.0, None, ALU.mult).then_inc(neg_max_ready, 1)

            def mix_maps(n, hp):
                dve.wait_ge(exps_done, 4 * n + 4)
                dve.reciprocal(inv_sum[:, :], row_sum[:, :]).then_inc(mix, 1)
                dve.wait_ge(mix, 4 * n + 1)
                dve.tensor_scalar(neg_lam_inv[:, :], inv_sum[:, 2:4], neg_lam[:, 0:1], None, ALU.mult).then_inc(mix, 1)
                dve.wait_ge(mix, 4 * n + 2)
                for t, (a, b) in enumerate(((0, P), (P, 384))):
                    dve.tensor_scalar(probs[:, 1, a:b], probs[:, 1, a:b], neg_lam_inv[:, t:t + 1], None,
                                      ALU.mult).then_inc(mix, 1)
                dve.wait_ge(mix, 4 * n + 4)
                if hp:
                    dve.wait_ge(mixed_turned, n)
                for t, (a, b) in enumerate(((0, P), (P, 384))):
                    m = dve.scalar_tensor_tensor(out=mixed[:, a:b], in0=probs[:, 0, a:b], scalar=inv_sum[:, t:t + 1],
                                                 in1=probs[:, 1, a:b], op0=ALU.mult, op1=ALU.add)
                m.then_inc(mixed_ready, 1)

            def normalise(n, hp):
                dve.wait_ge(sq_done, 2 * n + 2)
                dve.tensor_scalar(rms_rstd[:, hp, 0, :], sq_sum[:, hp, :], 1.0 / SEQ, RMS_EPS,
                                  ALU.mult, ALU.add).then_inc(ms_ready, 1)
                dve.wait_ge(rms_pow, n + 1)
                for t in range(TB):
                    dve.scalar_tensor_tensor(out=o_norm[:, hp, t, :], in0=ps[:, 5 + hp, t * SEQ:(t + 1) * SEQ],
                                             scalar=rms_rstd[:, hp, 1, t:t + 1], in1=subln,
                                             op0=ALU.mult, op1=ALU.mult).then_inc(o_normed, 1)

            def o_lo_head(n, hp):
                dve.wait_ge(o_hi, n + 1)
                dve.tensor_tensor(F[:, bass.ds(2 * n, 2), 1, :],
                                  ps[:, 7 - 2 * hp, :].rearrange("p (e t) -> p e t", e=2),
                                  F[:, bass.ds(2 * n, 2), 0, :].bitcast(F32), ALU.subtract).then_inc(o_lo, 1)

            def add_halves(n, par, dst, scale=None):
                for s in range(2):
                    dve.wait_ge(half_copied, 2 * n + (s + 1))
                    b = 4 * par + 2 * s
                    left = ps[:, b:b + 2, 0:SEQ]
                    if scale is None:
                        dve.tensor_tensor(dst[:, 2 * s:2 * s + 2, :], left, qk_half, ALU.add).then_inc(halves_added, 1)
                    else:
                        dve.scalar_tensor_tensor(out=dst[:, 2 * s:2 * s + 2, :], in0=left, scalar=scale, in1=qk_half,
                                                 op0=ALU.mult, op1=ALU.add).then_inc(halves_added, 1)

            def v_window(g, c):
                softmax_max(2 * c, 0)
                mix_maps(2 * c, 0)
                split_lo(g + 1, 0)
                softmax_max(2 * c + 1, 1)
                split_lo(g + 1, 1)
                mix_maps(2 * c + 1, 1)
                split_lo(g + 1, 2)
                split_lo(g + 1, 3)

            split_all(1)
            add_halves(0, 0, qT, Q_SCALE)
            split_all(2)
            add_halves(1, 1, kT)
            with dve.Fori(0, PAIRS - 1) as c:
                v_window(3 * c + 2, c)
                g = 3 * c + 3
                split_lo(g + 1, 0)
                normalise(2 * c, 0)
                split_lo(g + 1, 1)
                normalise(2 * c + 1, 1)
                split_lo(g + 1, 2)
                o_lo_head(2 * c, 0)
                o_lo_head(2 * c + 1, 1)
                split_lo(g + 1, 3)
                add_halves(2 * c + 2, 0, qT, Q_SCALE)
                split_all(g + 2)
                add_halves(2 * c + 3, 1, kT)
            c = PAIRS - 1
            v_window(3 * c + 2, c)
            normalise(2 * c, 0)
            normalise(2 * c + 1, 1)
            o_lo_head(2 * c, 0)
            o_lo_head(2 * c + 1, 1)

            def stats_of(t, q, r, static):
                dve.wait_ge(res_added, 2 * r + (t + 1))
                if static:
                    dve.bn_stats(ln_stats[:, t, q, :], res[:, t, q * COLS:(q + 1) * COLS]).then_inc(ln_dve, 1)
                else:
                    dve.bn_stats(ln_stats[:, t, bass.ds(q, 1), :].rearrange("p a b -> p (a b)"),
                                 res[:, t, bass.ds(COLS * q, COLS)]).then_inc(ln_dve, 1)

            def out_window(g, q, r, rows, with_stats, static=False):
                add_residual(0, COLS * q, (first_block_done, rows + 1))
                if with_stats:
                    stats_of(0, q, r, static)
                split_all(g + 1)
                add_residual(1, COLS * q, (w_used, 4 * g + 4))
                if with_stats:
                    stats_of(1, q, r, static)

            LN_STEPS = 2 * QUARTERS + TB * (1 + QUARTERS)

            def ln_block(L, t):
                at = LN_STEPS * (L - 1) + (2 * QUARTERS - 1 + t) + t * (1 + QUARTERS)
                dve.wait_ge(ln_dve, at)
                dve.bn_aggr(ln_mean_var[:, t, :], ln_stats[:, t].rearrange("p a b -> p (a b)")).then_inc(ln_dve, 1)
                dve.wait_ge(ln_dve, at + 1)
                dve.tensor_scalar(ln_rstd[:, t, 0:1], ln_mean_var[:, t, 1:2], LN_EPS, None,
                                  ALU.add).then_inc(ln_var, 1)
                dve.wait_ge(gb_loaded, 32 * L)
                for q in range(QUARTERS):
                    c = slice(q * COLS, (q + 1) * COLS)
                    dve.scalar_tensor_tensor(out=res[:, t, c], in0=res[:, t, c], scalar=ln_mean_var[:, t, 0:1],
                                             in1=ln_gb[:, 0, c], op0=ALU.subtract, op1=ALU.mult).then_inc(ln_dve, 1)
                dve.wait_ge(ln_pow, 2 * (L - 1) + t + 1)
                for q in range(QUARTERS):
                    c = slice(q * COLS, (q + 1) * COLS)
                    dve.wait_ge(ln_dve, at + 2 + q)
                    dve.scalar_tensor_tensor(out=res[:, t, c], in0=res[:, t, c], scalar=ln_rstd[:, t, 1:2],
                                             in1=ln_gb[:, 1, c], op0=ALU.mult, op1=ALU.add).then_inc(ln_quarter, 1)

            def ln_window(g, r, rows, L):
                q = QUARTERS - 1
                add_residual(0, COLS * q, (first_block_done, rows + 1))
                stats_of(0, q, r, True)
                ln_block(L, 0)
                if L < 4:
                    split_lo(g + 1, 0)
                    x_lo_quarter(L, 0)
                    split_lo(g + 1, 1)
                    x_lo_quarter(L, 1)
                    x_lo_quarter(L, 2)
                    split_lo(g + 1, 2)
                add_residual(1, COLS * q, (w_used, 4 * g + 4))
                stats_of(1, q, r, True)
                if L < 4:
                    x_lo_quarter(L, 3)
                ln_block(L, 1)
                if L < 4:
                    for i in range(QUARTERS, TB * QUARTERS):
                        x_lo_quarter(L, i)
                    split_lo(g + 1, 3)

            dve.wait_ge(res_scaled, 8)
            out_window(G_WO, 0, 0, ROWS_WO, True, True)
            with dve.Fori(1, QUARTERS - 1) as q:
                out_window(q + G_WO, q, q, q + ROWS_WO, True)
            ln_window(G_WO + 3, 3, ROWS_WO + 3, 1)

            def up_window(g, n, par, k, fk):
                split_all(g + 1)
                dve.wait_ge(lo_ready, 4 * g + 8)
                for s in range(2):
                    dve.wait_ge(half_copied, 2 * n + (s + 1))
                    b = 4 * par + 2 * s
                    dve.tensor_tensor(mlp_hidden[:, s], ps[:, b:b + 2, 0:SEQ], mlp_half[:, s], ALU.add
                                      ).then_inc(halves_added, 1)
                for s in range(2):
                    dve.wait_ge(halves_added, 2 * n + (s + 1))
                    dve.scalar_tensor_tensor(out=mlp_hidden[:, s], in0=mlp_hidden[:, s], scalar=0.0,
                                             in1=mlp_hidden[:, s], op0=ALU.max, op1=ALU.mult).then_inc(squared, 1)
                for s in range(2):
                    dve.wait_ge(f_hi, k + (s + 1))
                    dve.tensor_tensor(F[:, bass.ds(fk + 2 * s, 2), 1, :], mlp_hidden[:, s],
                                      F[:, bass.ds(fk + 2 * s, 2), 0, :].bitcast(F32), ALU.subtract
                                      ).then_inc(f_lo, 1)

            def mlp(m, L):
                g0, n0, r0, w0 = G_MLP[m], COLS_MLP[m], RES_MLP[m], ROWS_MLP[m]
                with dve.Fori(0, CHUNKS - 1) as ch:
                    with dve.Fori(0, 2) as p:
                        for e in range(2):
                            up_window(8 * ch + 2 * p + (g0 + e), 4 * ch + 2 * p + (n0 + e), e,
                                      8 * ch + 4 * p + (32 * m + 2 * e), 8 * p + 4 * e)
                    dve.wait_ge(res_scaled, 8 * (L + 1))
                    with dve.Fori(0, 4) as q:
                        out_window(8 * ch + q + (g0 + 4), q, 4 * ch + q + r0, 4 * ch + q + w0, False)
                ch = CHUNKS - 1
                with dve.Fori(0, 2) as p:
                    for e in range(2):
                        up_window(2 * p + (g0 + e + 8 * ch), 2 * p + (n0 + e + 4 * ch), e,
                                  4 * p + (32 * m + 2 * e + 8 * ch), 8 * p + 4 * e)
                with dve.Fori(0, 3) as q:
                    out_window(q + (g0 + 8 * ch + 4), q, q + (r0 + 4 * ch), q + (w0 + 4 * ch), True)
                ln_window(g0 + 8 * ch + 7, r0 + 4 * ch + 3, w0 + 4 * ch + 3, L + 1)

            mlp(0, 1)

            dve.wait_ge(z_half_copied, 1)
            dve.tensor_tensor(zT[0:RANK, :], ps[0:RANK, 4, 0:SEQ], z_half[0:RANK, :], ALU.add).then_inc(zT_ready, 1)
            split_lo(G_GLA + 1, 0)
            dve.wait_ge(gk_act, 4)
            dve.scalar_tensor_tensor(out=gate, in0=gate, scalar=0.0, in1=gk_tmp, op0=ALU.min, op1=ALU.subtract
                                     ).then_inc(gate_ready, 1)
            dve.wait_ge(gate_ready, 1)
            dve.wait_ge(consts_ready, 8)
            for i in range(GLA_HEADS * DKT):
                dve.tensor_tensor_scan(cum[:, i, :], scan_mask, gate[:, i, :], 0.0, ALU.mult, ALU.add
                                       ).then_inc(scanned, 1)
            dve.wait_ge(scanned, 8)
            cc = cum.rearrange("p i (c t) -> p i c t", t=CHUNK)
            dve.tensor_tensor(to_last, cc[:, :, 0:3, CHUNK - 1:CHUNK].to_broadcast([P, GLA_HEADS * DKT, 3, CHUNK]),
                              cc[:, :, 0:3, :], ALU.subtract).then_inc(to_last_ready, 1)
            for j in range(1, TILES):
                split_lo(G_GLA + 1, j)

            def gla_q(u):
                n = COLS_GLA + u
                if u:
                    dve.wait_ge(q_ready, 2 * u)
                for s in range(2):
                    dve.wait_ge(half_copied, 2 * n + s + 1)
                    b = 4 * (u % 2) + 2 * s
                    dve.tensor_tensor(gla_qk[:, s], ps[:, b:b + 2, 0:SEQ], gla_half[:, s], ALU.add
                                      ).then_inc(halves_added, 1)
                dve.wait_ge(decays_ready, 1)
                for s in range(2):
                    dve.wait_ge(halves_added, 2 * n + s + 1)
                    qd = G[:, 2 * u + s, :, G_QD, :]
                    dve.scalar_tensor_tensor(out=qd, in0=gla_qk[:, s], scalar=GLA_Q_SCALE, in1=qd,
                                             op0=ALU.mult, op1=ALU.mult).then_inc(q_ready, 1)

            def gla_k(u):
                n = COLS_GLA + 2 + u
                dve.wait_ge(q_ready, 4)
                if u:
                    dve.wait_ge(key_step, 16 * u)
                for s in range(2):
                    dve.wait_ge(half_copied, 2 * n + s + 1)
                    b = 4 * (u % 2) + 2 * s
                    dve.tensor_tensor(gla_qk[:, s], ps[:, b:b + 2, 0:SEQ], gla_half[:, s], ALU.add
                                      ).then_inc(halves_added, 1)
                dve.wait_ge(decays_ready, 5)
                for s in range(2):
                    h = 2 * u + s
                    step = 8 * h
                    dve.wait_ge(halves_added, 2 * n + s + 1)
                    k = gla_qk[:, s]
                    k4 = k.rearrange("p e (b c t) -> p e b c t", b=2, c=2)
                    inv = G[:, h, :, G_KI, :]
                    inv4 = inv.rearrange("p e (b c t) -> p e b c t", b=2, c=2)
                    d4 = G[:, h, :, G_D, :].rearrange("p e (b c t) -> p e b c t", b=2, c=2)
                    r = G[:, h, :, G_R, :]
                    dve.tensor_tensor(inv, inv, k, ALU.mult).then_inc(key_step, 1)
                    dve.tensor_tensor(d4[:, :, :, 0, :], d4[:, :, :, 0, :], k4[:, :, :, 0, :], ALU.mult
                                      ).then_inc(key_step, 1)
                    dve.tensor_tensor(r[:, :, CHUNK:P], r[:, :, CHUNK:P], k[:, :, CHUNK:P], ALU.mult
                                      ).then_inc(key_step, 1)
                    dve.wait_ge(key_step, step + 3)
                    dve.tensor_copy(d4[:, :, :, 1, :], inv4[:, :, :, 1, :]).then_inc(key_step, 1)
                    for e in range(DKT):
                        dve.tensor_scalar(r[:, e, 0:CHUNK], G[:, h, e, G_D, 0:CHUNK],
                                          chunk_decay[:, 2 * h + e, 0:1], None, ALU.mult).then_inc(key_step, 1)
                    dve.wait_ge(key_step, step + 6)
                    for e in range(DKT):
                        dve.tensor_scalar(r[:, e, P:2 * P], r[:, e, 0:P],
                                          chunk_decay[:, 2 * h + e, 1:2], None, ALU.mult).then_inc(key_step, 1)

            gla_q(0)
            split_all(G_GLA + 2)
            gla_q(1)
            split_all(G_GLA + 3)
            gla_k(0)
            split_all(G_GLA + 4)
            gla_k(1)
            split_all(G_VR + 1)

            def gate_r_block(h, t):
                dve.wait_ge(exp_r, 2 * h + (t + 1))
                dve.tensor_scalar(sig, sig, 1.0, None, ALU.add).then_inc(sig_step, 1)
                dve.wait_ge(sig_step, 4 * h + (2 * t + 1))
                dve.reciprocal(sig, sig).then_inc(sig_step, 1)
                dve.wait_ge(sig_step, 4 * h + (2 * t + 2))
                dve.tensor_tensor(silu_r[:, t, :], ps[:, 4 * t, :], sig, ALU.mult).then_inc(r_gated, 1)

            def r_window(h):
                gate_r_block(h, 0)
                split_lo(2 * h + (G_VR + 2), 0)
                dve.wait_ge(gsq_done, 2 * h + 2)
                dve.tensor_scalar(rms_rstd[:, 0, 0, :], sq_sum[:, 0, :], 1.0 / DV, RMS_EPS,
                                  ALU.mult, ALU.add).then_inc(gms_ready, 1)
                for j in range(1, TILES):
                    split_lo(2 * h + (G_VR + 2), j)
                gate_r_block(h, 1)
                dve.wait_ge(grms_pow, h + 1)
                for t in range(TB):
                    dve.wait_ge(r_gained, 2 * h + (t + 1))
                    dve.scalar_tensor_tensor(out=gla_o[:, t, :], in0=ps[:, 2 + t, :], scalar=rms_rstd[:, 0, 1, t:t + 1],
                                             in1=silu_r[:, t, :], op0=ALU.mult, op1=ALU.mult).then_inc(go_normed, 1)

            def o_lo_gla(h, t):
                dve.wait_ge(go_hi, 2 * h + (t + 1))
                dve.tensor_tensor(F[:, bass.ds(4 * h, 4), 1, blk(t)],
                                  ps[:, 5 + t, :].rearrange("p (e t) -> p e t", t=P),
                                  F[:, bass.ds(4 * h, 4), 0, blk(t)].bitcast(F32), ALU.subtract).then_inc(go_lo, 1)

            with dve.Fori(0, GLA_HEADS - 1) as h:
                r_window(h)
                o_lo_gla(h, 0)
                o_lo_gla(h, 1)
                split_all(2 * h + (G_VR + 3))
            h = GLA_HEADS - 1
            r_window(h)
            o_lo_gla(h, 0)
            o_lo_gla(h, 1)
            dve.wait_ge(res_scaled, 24)
            out_window(G_GWO, 0, RES_GWO, ROWS_GWO, True, True)
            with dve.Fori(1, QUARTERS - 1) as q:
                out_window(q + G_GWO, q, q + RES_GWO, q + ROWS_GWO, True)
            ln_window(G_GWO + 3, RES_GWO + 3, ROWS_GWO + 3, 3)
            mlp(1, 3)


_INS = ["x", "attn_w_qkv", "attn_w_o", "attn_lambda", "attn_subln", "gla_w_in", "gla_w_gk2", "gla_b_gk",
        "gla_norm", "gla_w_o", "mlp_w1", "mlp_w2", "ln_g", "ln_b"]
_OUTS = [((1, SEQ, D), "float32")]


def kernel(**inputs):
    import numpy as _np
    import concourse.bacc as _bacc
    from concourse import mybir as _mybir
    from concourse.bass_utils import run_bass_kernel_spmd as _run

    nc = _bacc.Bacc("TRN2", target_bir_lowering=False, num_devices=1)
    arrays, args = {}, []
    for name in _INS:
        a = _np.ascontiguousarray(inputs[name])
        arrays[f"in_{name}_dram"] = a
        args.append(nc.dram_tensor(f"in_{name}_dram", a.shape, _mybir.dt.from_np(a.dtype), kind="ExternalInput").ap())
    for i, (shape, dtype) in enumerate(_OUTS):
        dt = _mybir.dt.from_np(_np.dtype(dtype))
        args.append(nc.dram_tensor(f"out_{i}_dram", shape, dt, kind="ExternalOutput").ap())
    build(nc, *args)
    r = _run(nc, [arrays], core_ids=[0])
    got = tuple(r.results[0][f"out_{i}_dram"] for i in range(len(_OUTS)))
    return got[0]
```

```python
import math
from contextlib import ExitStack

import concourse.bass as bass
from concourse import mybir

F32 = mybir.dt.float32
F32R = mybir.dt.float32r
ALU = mybir.AluOpType
ACT = mybir.ActivationFunctionType

P = 128
D = 2048
SEQ = 256
TB = SEQ // P
KT = D // P
COLS = 512
TILES = 4
KPT = KT // TILES
QUARTERS = D // COLS
DEPTH = 2
FF = 4 * D
CHUNKS = FF // D
CHUNK = 64

HEADS = 8
DH = 128
PAIRS = HEADS // 2
LAM_INIT = 0.8 - 0.6 * math.exp(-0.3 * 0)
Q_SCALE = DH ** -0.5
MASKED = -3.0e38

GLA_HEADS = 4
KEY = D // 2
DK = KEY // GLA_HEADS
DKT = DK // P
DV = D // GLA_HEADS
RANK = 16
TAU = 16.0
GLA_Q_SCALE = DK ** -0.5

ALPHA = (2.0 * DEPTH) ** 0.25
LN_EPS = 1e-5
RMS_EPS = 1e-6

G_WO = 3 * PAIRS
G_MLP = [G_WO + QUARTERS, 0]
G_GLA = G_MLP[0] + 8 * CHUNKS
G_VR = G_GLA + 4
G_GWO = G_VR + 2 * GLA_HEADS
G_MLP[1] = G_GWO + QUARTERS
COLS_MLP = [2 * PAIRS, 2 * PAIRS + 4 * CHUNKS + 4]
COLS_GLA = 2 * PAIRS + 4 * CHUNKS
RES_MLP = [QUARTERS, 2 * QUARTERS + 4 * CHUNKS]
RES_GWO = QUARTERS + 4 * CHUNKS
ROWS_WO = PAIRS
ROWS_MLP = [ROWS_WO + QUARTERS, 0]
ROWS_VR = ROWS_MLP[0] + 4 * CHUNKS
ROWS_GWO = ROWS_VR + 2 * GLA_HEADS
ROWS_MLP[1] = ROWS_GWO + QUARTERS
LN_BANKS = (5, 6, 7)


def build(nc, x, attn_w_qkv, attn_w_o, attn_lambda, attn_subln, gla_w_in, gla_w_gk2, gla_b_gk,
          gla_norm, gla_w_o, mlp_w1, mlp_w2, ln_g, ln_b, out):
    ctx = ExitStack()
    with ctx:
        def sb(name, shape, dt=F32):
            return ctx.enter_context(nc.sbuf_tensor(name, shape, dt))

        def sem(name):
            return ctx.enter_context(nc.semaphore(name))

        raw = sb("raw", [P, TILES, KPT, COLS])
        hi = sb("hi", [P, TILES, KPT, COLS], F32R)
        lo = sb("lo", [P, TILES, KPT, COLS], F32R)
        X = sb("X", [P, KT, 2, SEQ], F32R)
        res = sb("res", [P, TB, D])
        f_bytes = KT * 2 * SEQ * 4
        f_at = nc.sbuf_base
        F_hold = sb("F_hold", [P, f_bytes // 4])
        F = nc.alloc_sbuf_tensor_at("F", [P, KT, 2, SEQ], F32R, offset=f_at)
        G = nc.alloc_sbuf_tensor_at("G", [P, GLA_HEADS, DKT, 4, SEQ], F32, offset=f_at)
        G_QD, G_KI, G_D, G_R = range(4)
        wz_hi = sb("wz_hi", [P, KT, RANK], F32R)
        wz_lo = sb("wz_lo", [P, KT, RANK], F32R)
        work = sb("work", [P, 7168])
        ident = sb("ident", [P, P])
        b_gk = sb("b_gk", [P, KEY // P])
        ln_stats = sb("ln_stats", [P, TB, QUARTERS, 6])
        ln_mean_var = sb("ln_mean_var", [P, TB, 2])
        ln_rstd = sb("ln_rstd", [P, TB, 2])
        minus_half = sb("minus_half", [P, 2])
        row_max = sb("row_max", [P, 4])
        neg_max = sb("neg_max", [P, 4])
        row_sum = sb("row_sum", [P, 4])
        inv_sum = sb("inv_sum", [P, 4])
        neg_lam_inv = sb("neg_lam_inv", [P, 2])
        lam_parts = sb("lam_parts", [P, 4])
        neg_lam = sb("neg_lam", [P, 1])
        sq_sum = sb("sq_sum", [P, 2, 2])
        rms_rstd = sb("rms_rstd", [P, 2, 2, 2])
        chunk_decay = sb("chunk_decay", [P, GLA_HEADS * DKT, 2])

        def part(at, *dims):
            n = math.prod(dims)
            v = work[:, at:at + n]
            if len(dims) == 1:
                return v
            names = "abc"[:len(dims)]
            return v.rearrange(f"p ({' '.join(names)}) -> p {' '.join(names)}",
                               **{k: d for k, d in zip(names, dims)})

        ln_gb = part(0, 2, D)
        mlp_half = part(4096, 2, 2, SEQ)
        mlp_hidden = part(5120, 2, 2, SEQ)
        qT = part(0, 4, SEQ)
        kT = part(1024, 4, SEQ)
        v_rows = part(2048, TB, COLS)
        probs = part(3072, 2, 384)
        mixed = part(3840, 384)
        mixedT = part(4224, 2, 384)
        o_norm = part(4992, 2, 2, SEQ)
        mask = part(6016, 384)
        subln = part(6400, 256)
        qk_half = part(6656, 2, SEQ)
        lam_rows = part(4992, 4, DH)
        wz_raw = part(2048, KT, RANK)
        cum = part(0, GLA_HEADS * DKT, SEQ)
        gate = part(2048, GLA_HEADS * DKT, SEQ)
        gk_tmp = part(4096, GLA_HEADS * DKT, SEQ)
        to_last = part(4096, GLA_HEADS * DKT, 3, CHUNK)
        zT = part(4096, SEQ)
        w_gk2 = part(4352, KEY)
        z_half = part(5376, SEQ)
        scan_mask = part(6144, SEQ)
        gla_half = part(2048, 2, 2, SEQ)
        gla_qk = part(3072, 2, 2, SEQ)
        keys = part(0, DKT, 4, SEQ)
        gla_v = part(2048, TB, DV)
        silu_r = part(3072, TB, DV)
        sig = part(4096, DV)
        pairT = part(4608, 384)
        gla_o = part(4992, TB, DV)
        gla_gain = part(6016, DV)

        ps = ctx.enter_context(nc.psum_tensor("ps", [P, 8, COLS], F32))

        x_loaded = [sem(f"x_loaded{q}") for q in range(QUARTERS)]
        raw_full = [sem(f"raw_full{j}") for j in range(TILES)]
        small_loaded = sem("small_loaded")
        gb_loaded = sem("gb_loaded")
        gk2_loaded = sem("gk2_loaded")
        gain_loaded = sem("gain_loaded")
        out_stored = sem("out_stored")
        consts_ready = sem("consts_ready")
        hi_ready = sem("hi_ready")
        lo_ready = sem("lo_ready")
        w_used = sem("w_used")
        first_block_done = sem("first_block_done")
        half_copied = sem("half_copied")
        halves_added = sem("halves_added")
        res_added = sem("res_added")
        ln_dve = sem("ln_dve")
        ln_var = sem("ln_var")
        ln_pow = sem("ln_pow")
        ln_quarter = sem("ln_quarter")
        ln_turned = sem("ln_turned")
        x_hi = sem("x_hi")
        x_lo = sem("x_lo")
        res_scaled = sem("res_scaled")
        squared = sem("squared")
        f_hi = sem("f_hi")
        f_lo = sem("f_lo")
        set_up = sem("set_up")
        wz_hi_ready = sem("wz_hi_ready")
        lam_dots = sem("lam_dots")
        lam_exps = sem("lam_exps")
        v_copied = sem("v_copied")
        scores_done = sem("scores_done")
        scores_seen = sem("scores_seen")
        pairs_seen = sem("pairs_seen")
        maxes = sem("maxes")
        neg_max_ready = sem("neg_max_ready")
        exps_done = sem("exps_done")
        mix = sem("mix")
        mixed_ready = sem("mixed_ready")
        mixed_turned = sem("mixed_turned")
        mixedT_ready = sem("mixedT_ready")
        pv_done = sem("pv_done")
        sq_done = sem("sq_done")
        ms_ready = sem("ms_ready")
        rms_pow = sem("rms_pow")
        o_normed = sem("o_normed")
        o_turned = sem("o_turned")
        o_hi = sem("o_hi")
        o_lo = sem("o_lo")
        z_done = sem("z_done")
        z_half_copied = sem("z_half_copied")
        zT_ready = sem("zT_ready")
        gk_done = sem("gk_done")
        gk_act = sem("gk_act")
        gate_ready = sem("gate_ready")
        scanned = sem("scanned")
        to_last_ready = sem("to_last_ready")
        decays_ready = sem("decays_ready")
        q_ready = sem("q_ready")
        key_step = sem("key_step")
        keys_staged = sem("keys_staged")
        pairs_done = sem("pairs_done")
        pairs_copied = sem("pairs_copied")
        pairs_masked = sem("pairs_masked")
        go_done = sem("go_done")
        gsq_done = sem("gsq_done")
        gms_ready = sem("gms_ready")
        grms_pow = sem("grms_pow")
        exp_r = sem("exp_r")
        sig_step = sem("sig_step")
        r_gated = sem("r_gated")
        r_gained = sem("r_gained")
        go_normed = sem("go_normed")
        go_turned = sem("go_turned")
        go_hi = sem("go_hi")
        go_lo = sem("go_lo")

        w_qkv = attn_w_qkv[0].rearrange("(t p) n -> p t n", p=P)
        w_o = attn_w_o[0].rearrange("(t p) n -> p t n", p=P)
        w_in = gla_w_in[0].rearrange("(t p) n -> p t n", p=P)
        w_go = gla_w_o[0].rearrange("(t p) n -> p t n", p=P)
        w_1 = [mlp_w1[m].rearrange("(t p) n -> p t n", p=P) for m in range(DEPTH)]
        w_2 = [mlp_w2[m].rearrange("(t p) n -> p t n", p=P) for m in range(DEPTH)]
        x_rows = x[0].rearrange("(t p) n -> p t n", p=P)
        out_rows = out[0].rearrange("(t p) n -> p t n", p=P)

        def blk(t):
            return slice(t * P, (t + 1) * P)

        def place(L, i):
            return (i % TB, i // TB) if L == 0 else (i // QUARTERS, i % QUARTERS)

        block = ctx.enter_context(nc.Block())

        @block.sync
        def _(sp):
            def load_group(g, w, col, row=0):
                for j in range(TILES):
                    sp.wait_ge(lo_ready, 4 * g + j - 3)
                    sp.dma_start(raw[:, j], w[:, bass.ds(row + KPT * j, KPT), bass.ds(col, COLS)]
                                 ).then_inc(raw_full[j], 16)

            for q in range(QUARTERS):
                c = slice(q * COLS, (q + 1) * COLS)
                for t in range(TB):
                    sp.dma_start(res[:, t, c], x_rows[:, t, c]).then_inc(x_loaded[q], 16)
                sp.dma_start(raw[:, q], w_qkv[:, KPT * q:KPT * (q + 1), 0:COLS]).then_inc(raw_full[q], 16)
            load_group(1, w_qkv, D)
            with sp.Fori(0, PAIRS - 1) as c:
                load_group(3 * c + 2, w_qkv, 2 * D + COLS * c)
                load_group(3 * c + 3, w_qkv, COLS * c + COLS)
                load_group(3 * c + 4, w_qkv, COLS * c + (D + COLS))
            load_group(3 * PAIRS - 1, w_qkv, 2 * D + COLS * (PAIRS - 1))
            with sp.Fori(0, QUARTERS) as q:
                load_group(q + G_WO, w_o, COLS * q)

            def load_mlp(m):
                with sp.Fori(0, CHUNKS) as ch:
                    with sp.Fori(0, QUARTERS) as q:
                        load_group(8 * ch + q + G_MLP[m], w_1[m], D * ch + COLS * q)
                    with sp.Fori(0, QUARTERS) as q:
                        load_group(8 * ch + q + (G_MLP[m] + 4), w_2[m], COLS * q, KT * ch)

            load_mlp(0)
            with sp.Fori(0, 4) as q:
                load_group(q + G_GLA, w_in, COLS * q)
            with sp.Fori(0, GLA_HEADS) as h:
                load_group(2 * h + G_VR, w_in, COLS * h + 2 * KEY)
                load_group(2 * h + (G_VR + 1), w_in, COLS * h + (2 * KEY + D))
            with sp.Fori(0, QUARTERS) as q:
                load_group(q + G_GWO, w_go, COLS * q)
            load_mlp(1)
            for i in range(TB * QUARTERS):
                t, q = place(4, i)
                c = slice(q * COLS, (q + 1) * COLS)
                sp.wait_ge(ln_quarter, 8 * 3 + i + 1)
                sp.dma_start(out_rows[:, t, c], res[:, t, c]).then_inc(out_stored, 16)
            sp.wait_ge(out_stored, 16 * TB * QUARTERS)

        @block.gpsimd
        def _(pool):
            def load_gb(layer, i):
                for n, src in enumerate((ln_g, ln_b)):
                    pool.dma_start(ln_gb[:, n, :], src[layer, i].partition_broadcast(P)).then_inc(gb_loaded, 16)

            def scale_residual(L):
                for i in range(TB * QUARTERS):
                    t, q = place(L, i)
                    pool.wait_ge(ln_turned, 8 * L + i + 1)
                    r = res[:, t, q * COLS:(q + 1) * COLS]
                    pool.tensor_scalar(r, r, ALPHA, None, ALU.mult).then_inc(res_scaled, 1)

            def ln_powers(L):
                for t in range(TB):
                    pool.wait_ge(ln_var, 2 * (L - 1) + t + 1)
                    pool.tensor_tensor(ln_rstd[:, t, 1:2], ln_rstd[:, t, 0:1], minus_half[:, 0:1],
                                       ALU.pow).then_inc(ln_pow, 1)

            def rms_power(n, hp):
                pool.wait_ge(ms_ready, n + 1)
                pool.tensor_tensor(rms_rstd[:, hp, 1, :], rms_rstd[:, hp, 0, :], minus_half[:, :],
                                   ALU.pow).then_inc(rms_pow, 1)

            def gla_power(h):
                pool.wait_ge(gms_ready, h + 1)
                pool.tensor_tensor(rms_rstd[:, 0, 1, :], rms_rstd[:, 0, 0, :], minus_half[:, :],
                                   ALU.pow).then_inc(grms_pow, 1)

            pool.memset(ident[:, :], 0.0).then_inc(consts_ready, 1)
            pool.memset(mask, 0.0).then_inc(consts_ready, 1)
            pool.memset(minus_half[:, :], -0.5).then_inc(consts_ready, 1)
            pool.wait_ge(consts_ready, 3)
            pool.affine_select(out=ident[:, :], in_=ident[:, :], compare_op=ALU.not_equal, fill=1.0, base=0,
                               pattern=[[-1, P]], channel_multiplier=1).then_inc(consts_ready, 1)
            pool.memset(mask[0:CHUNK, CHUNK:P], MASKED).then_inc(consts_ready, 1)
            pool.memset(mask[0:CHUNK, 384 - CHUNK:384], MASKED).then_inc(consts_ready, 1)
            pool.dma_start(lam_rows.rearrange("p a b -> p (a b)"),
                           attn_lambda[0].rearrange("a b -> (a b)").partition_broadcast(P)).then_inc(small_loaded, 16)
            pool.dma_start(subln, attn_subln[0].partition_broadcast(P)).then_inc(small_loaded, 16)
            with nc.allow_non_contiguous_dma(reason="b_gk with a feature on each partition: 4 KB"):
                pool.dma_start(b_gk[:, :], gla_b_gk[0].rearrange("(t p) -> p t", p=P)).then_inc(small_loaded, 16)
            pool.dma_start(wz_raw, w_in[:, :, 2 * KEY + 2 * D:]).then_inc(small_loaded, 16)
            scale_residual(0)
            with pool.Fori(0, PAIRS) as c:
                rms_power(2 * c, 0)
                rms_power(2 * c + 1, 1)
            pool.wait_ge(o_turned, HEADS)
            load_gb(0, 0)
            ln_powers(1)
            scale_residual(1)
            pool.wait_ge(ln_quarter, 8)
            load_gb(0, 1)
            ln_powers(2)
            scale_residual(2)
            pool.wait_ge(ln_quarter, 16)
            pool.dma_start(w_gk2[0:RANK, :], gla_w_gk2[0]).then_inc(gk2_loaded, 16)
            sm = scan_mask.rearrange("p (c t) -> p c t", t=CHUNK)
            pool.memset(scan_mask, 1.0).then_inc(consts_ready, 1)
            pool.wait_ge(consts_ready, 7)
            pool.memset(sm[:, :, 0:1], 0.0).then_inc(consts_ready, 1)

            def stage_keys(h):
                if not isinstance(h, int) or h:
                    pool.wait_ge(pairs_done, h)
                pool.tensor_copy(part(0, 2048), G[:, bass.ds(h, 1)].rearrange("p h a b c -> p (h a b c)")
                                 ).then_inc(keys_staged, 1)

            def mask_pairs(h):
                pool.wait_ge(pairs_copied, h + 1)
                pool.sem_inc(pairs_seen, 1)
                d = pairT.rearrange("p (b t) -> p b t", t=P)[:, 0::2, :]
                pool.affine_select(out=d, in_=d, compare_op=ALU.is_ge, fill=0.0, base=0,
                                   pattern=[[0, 2], [1, P]], channel_multiplier=-1).then_inc(pairs_masked, 1)

            def gain_r(h):
                for t in range(TB):
                    pool.wait_ge(r_gated, 2 * h + t + 1)
                    pool.tensor_tensor(silu_r[:, t, :], silu_r[:, t, :], gla_gain, ALU.mult).then_inc(r_gained, 1)

            pool.wait_ge(key_step, 8 * GLA_HEADS)
            stage_keys(0)
            pool.dma_start(gla_gain, gla_norm[0].partition_broadcast(P)).then_inc(gain_loaded, 16)
            pool.wait_ge(gain_loaded, 16)
            with pool.Fori(0, GLA_HEADS - 1) as h:
                mask_pairs(h)
                stage_keys(h + 1)
                gla_power(h)
                gain_r(h)
            mask_pairs(GLA_HEADS - 1)
            gla_power(GLA_HEADS - 1)
            gain_r(GLA_HEADS - 1)
            pool.wait_ge(go_turned, 2 * GLA_HEADS)
            load_gb(1, 0)
            ln_powers(3)
            scale_residual(3)
            pool.wait_ge(ln_quarter, 24)
            load_gb(1, 1)
            ln_powers(4)

        @block.tensor
        def _(pe):
            def mm(o, w, m, start, stop):
                return pe.matmul(o, w, m, start=start, stop=stop)

            def rows_pass(g, t, acts, after=None):
                acc = ps[:, 4 * t, :]
                for j in range(TILES):
                    if t == 0:
                        pe.wait_ge(lo_ready, 4 * g + j + 1)
                    for k in range(KPT):
                        a = 4 * j + k
                        first, last = a == 0, a == KT - 1
                        mm(acc, acts[:, a, 0, blk(t)], hi[:, j, k, :], first, False)
                        mm(acc, acts[:, a, 0, blk(t)], lo[:, j, k, :], False, False)
                        m = mm(acc, acts[:, a, 1, blk(t)], hi[:, j, k, :], False, last)
                    if t == 1:
                        m.then_inc(w_used, 1)
                    elif j == TILES - 1:
                        m.then_inc(first_block_done, 1)
                    if after and (t, j) in after:
                        after[t, j]()

            def rows_late(g, acts, ready, bank_free, after=None):
                for t, tiles in ((0, (0, 1, 2)), (1, (0, 1, 2)), (0, (3,)), (1, (3,))):
                    for j in tiles:
                        if j == 0:
                            pe.wait_ge(*bank_free[t])
                        if t == 0:
                            pe.wait_ge(lo_ready, 4 * g + j + 1)
                            pe.wait_ge(*ready(j))
                        acc = ps[:, 4 * t, :]
                        for k in range(KPT):
                            a = 4 * j + k
                            mm(acc, acts[:, a, 0, blk(t)], hi[:, j, k, :], a == 0, False)
                            mm(acc, acts[:, a, 0, blk(t)], lo[:, j, k, :], False, False)
                            m = mm(acc, acts[:, a, 1, blk(t)], hi[:, j, k, :], False, a == KT - 1)
                        if t == 1:
                            m.then_inc(w_used, 1)
                        elif j == TILES - 1:
                            m.then_inc(first_block_done, 1)
                        if after and (t, j) in after:
                            after[t, j]()

            def cols_group(g, par, acts, after=None):
                for j in range(TILES):
                    pe.wait_ge(lo_ready, 4 * g + j + 1)
                    for k in range(KPT):
                        a = 4 * j + k
                        first, last = a == 0, a == KT - 1
                        for i in range(4):
                            acc = ps[:, 4 * par + i, :]
                            if first:
                                mm(acc, hi[:, j, k, blk(i)], acts[:, a, :, :], True, False)
                            m = mm(acc[:, 0:SEQ], lo[:, j, k, blk(i)], acts[:, a, 0, :], False, False)
                            if not first:
                                m = mm(acc, hi[:, j, k, blk(i)], acts[:, a, :, :], False, last)
                        if k == KPT - 1:
                            m.then_inc(w_used, 1)
                        if after and (j, k) in after:
                            after[j, k]()

            def turn_quarter(L, i):
                t, q = place(L, i)
                if L:
                    pe.wait_ge(ln_quarter, 8 * (L - 1) + i + 1)
                elif t == 0:
                    pe.wait_ge(x_loaded[q], 16 * TB)
                if i >= len(LN_BANKS):
                    pe.wait_ge(x_lo, 8 * L + i + 1 - len(LN_BANKS))
                for b in range(QUARTERS):
                    m = pe.transpose(ps[:, LN_BANKS[i % 3], blk(b)], res[:, t, blk(4 * q + b)], ident[:, :])
                m.then_inc(ln_turned, 1)

            def cols_by_block(g, L, after=None):
                turn = {(0, 1, 3): 4, (0, 3, 0): 5, (1, 0, 1): 6, (1, 1, 1): 7}
                for t in range(TB):
                    for j in range(TILES):
                        if t == 0:
                            pe.wait_ge(hi_ready, 4 * g + j + 1)
                        else:
                            pe.wait_ge(lo_ready, 4 * g + j + 1)
                        pe.wait_ge(x_lo, 8 * L + QUARTERS * t + j + 1)
                        for k in range(KPT):
                            a = 4 * j + k
                            for i in range(4):
                                acc = ps[:, i, :].rearrange("p (s t) -> p s t", s=2)
                                m = mm(acc[:, :, blk(t)], hi[:, j, k, blk(i)], X[:, a, :, blk(t)], t == 0 and a == 0, False)
                                if t:
                                    m = mm(acc[:, 0, :], lo[:, j, k, blk(i)], X[:, a, 0, :], False, a == KT - 1)
                            if t == 1 and k == KPT - 1:
                                m.then_inc(w_used, 1)
                            if (t, j, k) in turn:
                                turn_quarter(L, turn[t, j, k])
                            if after and (t, j, k) in after:
                                after[t, j, k]()

            def first_group():
                turn = {(0, 0): 2, (0, 1): 3, (1, 0): 4, (1, 1): 5, (2, 0): 6, (2, 1): 7}
                for j in range(TILES):
                    pe.wait_ge(hi_ready, j + 1)
                    pe.wait_ge(x_lo, 2 * j + 2)
                    for k in range(KPT):
                        a = 4 * j + k
                        for i in range(4):
                            mm(ps[:, i, :], hi[:, j, k, blk(i)], X[:, a, :, :], a == 0, False)
                        if (j, k) in turn:
                            turn_quarter(0, turn[j, k])
                    pe.wait_ge(lo_ready, j + 1)
                    for k in range(KPT):
                        a = 4 * j + k
                        for i in range(4):
                            m = mm(ps[:, i, 0:SEQ], lo[:, j, k, blk(i)], X[:, a, 0, :], False, a == KT - 1)
                    m.then_inc(w_used, 1)

            pe.wait_ge(consts_ready, 4)
            turn_quarter(0, 0)
            turn_quarter(0, 1)

            def scores(n, hp, c):
                pe.wait_ge(halves_added, 4 * c + 4)
                if hp:
                    pe.wait_ge(maxes, 4 * n)
                for s in range(2):
                    i = 2 * hp + s
                    mm(ps[:, 1 + s, 0:P], qT[:, i, blk(0)], kT[:, i, blk(0)], True, True)
                    m = mm(ps[:, 1 + s, P:P + SEQ], qT[:, i, blk(1)], kT[:, i, :], True, True)
                m.then_inc(scores_done, 1)

            def turn_mixed(n, hp):
                pe.wait_ge(mixed_ready, n + 1)
                for b in range(3):
                    m = pe.transpose(ps[:, 3 + 4 * hp, blk(b)], mixed[:, blk(b)], ident[:, :])
                m.then_inc(mixed_turned, 1)

            def weigh_values(n, hp, c):
                pe.wait_ge(mixedT_ready, n + 1)
                pe.wait_ge(v_copied, 2 * c + 2)
                o, col = ps[:, 5 + hp, :], slice(hp * SEQ, (hp + 1) * SEQ)
                mm(o[:, 0:SEQ], mixedT[:, hp, blk(0)], v_rows[:, 0, col], True, True)
                mm(o[:, SEQ:], mixedT[:, hp, blk(1)], v_rows[:, 0, col], True, False)
                mm(o[:, SEQ:], mixedT[:, hp, blk(2)], v_rows[:, 1, col], False, True).then_inc(pv_done, 1)

            def turn_output(n, hp):
                pe.wait_ge(o_normed, 2 * n + 2)
                if hp == 0:
                    pe.wait_ge(mixedT_ready, n + 2)
                bank = ps[:, 7 - 2 * hp, :]
                for e in range(2):
                    for t in range(TB):
                        m = pe.transpose(bank[:, e * SEQ + t * P:e * SEQ + (t + 1) * P],
                                         o_norm[:, hp, t, blk(e)], ident[:, :])
                m.then_inc(o_turned, 1)

            def v_group(g, c):
                pe.wait_ge(halves_added, 4 * c + 2)
                rows_pass(g, 0, X, {(0, 1): lambda: scores(2 * c, 0, c)})
                pe.wait_ge(halves_added, 4 * c + 4)
                rows_pass(g, 1, X, {(1, 0): lambda: scores(2 * c + 1, 1, c), (1, 1): lambda: turn_mixed(2 * c, 0)})

            first_group()
            pe.wait_ge(x_lo, 8)
            cols_group(1, 1, X)
            with pe.Fori(0, PAIRS - 1) as c:
                v_group(3 * c + 2, c)
                pe.wait_ge(v_copied, 2 * c + 1)
                pe.wait_ge(maxes, 8 * c + 8)
                pe.wait_ge(mixedT_ready, 2 * c + 1)
                cols_group(3 * c + 3, 0, X, {
                    (0, 3): lambda: (weigh_values(2 * c, 0, c), turn_mixed(2 * c + 1, 1)),
                    (1, 3): lambda: weigh_values(2 * c + 1, 1, c),
                    (2, 3): lambda: (turn_output(2 * c, 0), turn_output(2 * c + 1, 1))})
                pe.wait_ge(v_copied, 2 * c + 2)
                pe.wait_ge(o_lo, 2 * c + 2)
                cols_group(3 * c + 4, 1, X)
            c = PAIRS - 1
            v_group(3 * c + 2, c)
            rows_late(G_WO, F, lambda j: (o_lo, 2 * j + 2), ((v_copied, 2 * c + 1), (v_copied, 2 * c + 2)), {
                (0, 0): lambda: (weigh_values(2 * c, 0, c), turn_mixed(2 * c + 1, 1)),
                (0, 2): lambda: weigh_values(2 * c + 1, 1, c),
                (1, 0): lambda: turn_output(2 * c, 0), (1, 1): lambda: turn_output(2 * c + 1, 1)})

            def out_groups(g0, r0, n, acts):
                with pe.Fori(0, n) as q:
                    pe.wait_ge(res_added, 2 * q + (2 * r0 - 1))
                    rows_pass(q + g0, 0, acts)
                    pe.wait_ge(res_added, 2 * q + 2 * r0)
                    rows_pass(q + g0, 1, acts)

            def last_out_group(g, r, acts, L):
                pe.wait_ge(res_added, 2 * r - 1)
                rows_pass(g, 0, acts)
                pe.wait_ge(res_added, 2 * r)
                if L == 4:
                    rows_pass(g, 1, acts)
                    return
                rows_pass(g, 1, acts, {(1, 1): lambda: (turn_quarter(L, 0), turn_quarter(L, 1)),
                                       (1, 2): lambda: turn_quarter(L, 2), (1, 3): lambda: turn_quarter(L, 3)})

            out_groups(G_WO + 1, 1, QUARTERS - 2, F)
            last_out_group(G_WO + 3, 3, F, 1)

            def up_pair(m, L, g, n, r, first):
                pe.wait_ge(res_added, 2 * r - 1)
                pe.wait_ge(halves_added, 2 * n - 2)
                if first:
                    cols_by_block(g, L)
                    pe.wait_ge(x_lo, 8 * L + 8)
                else:
                    cols_group(g, 0, X)
                pe.wait_ge(res_added, 2 * r)
                pe.wait_ge(halves_added, 2 * n)
                cols_group(g + 1, 1, X)

            def down_first(m, ch, g, n, r):
                rows_late(g, F, lambda j: (f_lo, 8 * ch + (32 * m + 2 * j + 2)),
                          ((halves_added, 2 * n - 2), (halves_added, 2 * n)))

            def mlp(m, L):
                g0, n0, r0 = G_MLP[m], COLS_MLP[m], RES_MLP[m]
                up_pair(m, L, g0, n0, r0, True)
                up_pair(m, L, g0 + 2, n0 + 2, r0, False)
                down_first(m, 0, g0 + 4, n0 + 4, r0)
                out_groups(g0 + 5, r0 + 1, 3, F)
                with pe.Fori(1, CHUNKS - 1) as ch:
                    with pe.Fori(0, 2) as p:
                        up_pair(m, L, 8 * ch + 2 * p + g0, 4 * ch + 2 * p + n0, 4 * ch + r0, False)
                    down_first(m, ch, 8 * ch + (g0 + 4), 4 * ch + (n0 + 4), 4 * ch + r0)
                    with pe.Fori(0, 3) as q:
                        pe.wait_ge(res_added, 8 * ch + 2 * q + (2 * r0 + 1))
                        rows_pass(8 * ch + q + (g0 + 5), 0, F)
                        pe.wait_ge(res_added, 8 * ch + 2 * q + (2 * r0 + 2))
                        rows_pass(8 * ch + q + (g0 + 5), 1, F)
                ch = CHUNKS - 1
                with pe.Fori(0, 2) as p:
                    up_pair(m, L, 2 * p + (g0 + 8 * ch), 2 * p + (n0 + 4 * ch), r0 + 4 * ch, False)
                down_first(m, ch, g0 + 8 * ch + 4, n0 + 4 * ch + 4, r0 + 4 * ch)
                out_groups(g0 + 8 * ch + 5, r0 + 4 * ch + 1, 2, F)
                last_out_group(g0 + 8 * ch + 7, r0 + 4 * ch + 3, F, L + 1)

            mlp(0, 1)

            def gate_inputs():
                pe.wait_ge(x_lo, 24)
                pe.wait_ge(res_added, 2 * RES_GWO)
                z = ps[0:RANK, 4, :]
                for a in range(KT):
                    if a == 0:
                        mm(z, wz_hi[:, a, :], X[:, a, :, :], True, False)
                    m = mm(z[:, 0:SEQ], wz_lo[:, a, :], X[:, a, 0, :], False, False)
                    if a:
                        m = mm(z, wz_hi[:, a, :], X[:, a, :, :], False, a == KT - 1)
                m.then_inc(z_done, 1)

            def gate_scores():
                pe.wait_ge(zT_ready, 1)
                pe.wait_ge(gk2_loaded, 16)
                for i in range(KEY // P):
                    m = mm(ps[:, 4 + i // 2, (i % 2) * SEQ:(i % 2 + 1) * SEQ], w_gk2[0:RANK, blk(i)],
                           zT[0:RANK, :], True, True)
                m.then_inc(gk_done, 1)

            pe.wait_ge(res_added, 2 * RES_GWO - 1)
            cols_by_block(G_GLA, 2, {(1, 2, 1): gate_inputs, (1, 2, 3): gate_scores})
            pe.wait_ge(gk_act, 1)
            cols_group(G_GLA + 1, 1, X)
            pe.wait_ge(halves_added, 2 * COLS_GLA + 2)
            cols_group(G_GLA + 2, 0, X)
            pe.wait_ge(halves_added, 2 * COLS_GLA + 4)
            cols_group(G_GLA + 3, 1, X)

            def key_pairs(h):
                pe.wait_ge(keys_staged, h + 1)
                plan = [(0, 0, G_KI, 0), (1, 0, G_D, 0), (2, 0, G_R, 0), (2, 1, G_KI, P), (3, 0, G_R, P), (3, 1, G_D, P)]
                for chunk, sblk, kind, at in plan:
                    col = chunk * CHUNK if sblk == 0 else SEQ + (chunk - 2) * CHUNK
                    for e in range(DKT):
                        m = mm(ps[:, 1, col:col + CHUNK], keys[:, e, kind, at:at + P],
                               keys[:, e, G_QD, chunk * CHUNK:(chunk + 1) * CHUNK], e == 0, e == DKT - 1)
                m.then_inc(pairs_done, 1)

            def weigh_gla(h):
                pe.wait_ge(pairs_masked, h + 1)
                pe.wait_ge(v_copied, 2 * h + (2 * PAIRS + 2))
                mm(ps[:, 2, :], pairT[:, 0:P], gla_v[:, 0, :], True, True)
                mm(ps[:, 3, :], pairT[:, P:2 * P], gla_v[:, 0, :], True, False)
                mm(ps[:, 3, :], pairT[:, 2 * P:3 * P], gla_v[:, 1, :], False, True).then_inc(go_done, 1)

            def turn_gla(h, t):
                pe.wait_ge(go_normed, 2 * h + t + 1)
                for e in range(DV // P):
                    m = pe.transpose(ps[:, 5 + t, blk(e)], gla_o[:, t, blk(e)], ident[:, :])
                m.then_inc(go_turned, 1)

            def r_group(h):
                pe.wait_ge(v_copied, 2 * h + (2 * PAIRS + 1))
                rows_pass(2 * h + (G_VR + 1), 0, X, {(0, 0): lambda: key_pairs(h), (0, 3): lambda: weigh_gla(h)})
                pe.wait_ge(v_copied, 2 * h + (2 * PAIRS + 2))
                rows_pass(2 * h + (G_VR + 1), 1, X)

            pe.wait_ge(halves_added, 2 * COLS_GLA + 6)
            rows_pass(G_VR, 0, X)
            pe.wait_ge(halves_added, 2 * COLS_GLA + 8)
            rows_pass(G_VR, 1, X)
            with pe.Fori(0, GLA_HEADS - 1) as h:
                r_group(h)
                pe.wait_ge(r_gated, 2 * h + 1)
                rows_pass(2 * h + (G_VR + 2), 0, X, {(0, 3): lambda: turn_gla(h, 0)})
                pe.wait_ge(r_gated, 2 * h + 2)
                rows_pass(2 * h + (G_VR + 2), 1, X, {(1, 0): lambda: turn_gla(h, 1)})
            h = GLA_HEADS - 1
            r_group(h)
            rows_late(G_GWO, F, lambda j: (go_lo, 2 * j + 2), ((r_gated, 2 * h + 1), (r_gated, 2 * h + 2)), {
                (0, 2): lambda: turn_gla(h, 0), (1, 0): lambda: turn_gla(h, 1)})
            out_groups(G_GWO + 1, RES_GWO + 1, QUARTERS - 2, F)
            last_out_group(G_GWO + 3, RES_GWO + 3, F, 3)
            mlp(1, 3)

        @block.scalar
        def _(act):
            def split_hi(g, j):
                act.wait_ge(raw_full[j], 16 * g + 16)
                if not isinstance(g, int) or g:
                    act.wait_ge(w_used, 4 * g + j - 3)
                act.activation(hi[:, j], raw[:, j], ACT.Copy).then_inc(hi_ready, 1)

            def split_some(g, n):
                for j in range(n):
                    split_hi(g, j)

            def split_all(g):
                split_some(g, TILES)

            def copy_halves(g, n, par, dst, slots=2, scale=1.0):
                act.wait_ge(w_used, 4 * g + 4)
                for s in range(2):
                    if slots == 1:
                        if s or not isinstance(n, int) or n:
                            act.wait_ge(halves_added, 2 * n + s)
                    elif not isinstance(n, int) or n:
                        act.wait_ge(halves_added, 2 * n + s - 1)
                    b = 4 * par + 2 * s
                    d = dst if slots == 1 else dst[:, s]
                    act.activation(d, ps[:, b:b + 2, SEQ:], ACT.Copy, scale=scale).then_inc(half_copied, 1)

            def x_hi_quarter(L, i):
                t, q = place(L, i)
                act.wait_ge(ln_turned, 8 * L + i + 1)
                act.activation(X[:, 4 * q:4 * q + 4, 0, blk(t)],
                               ps[:, LN_BANKS[i % 3], :].rearrange("p (b t) -> p b t", t=P),
                               ACT.Copy).then_inc(x_hi, 1)

            for i in range(TB * QUARTERS):
                x_hi_quarter(0, i)
                if i % 2:
                    split_hi(0, i // 2)

            def exps(n, hp):
                act.wait_ge(neg_max_ready, n + 1)
                for s in range(2):
                    for t, (a, b) in enumerate(((0, P), (P, 384))):
                        i = 2 * s + t
                        act.activation(probs[:, s, a:b], probs[:, s, a:b], ACT.Exp, bias=neg_max[:, i:i + 1],
                                       accum_out=row_sum[:, i:i + 1]).then_inc(exps_done, 1)

            def copy_mixedT(n, hp):
                act.wait_ge(mixed_turned, n + 1)
                act.activation(mixedT[:, hp, :], ps[:, 3 + 4 * hp, 0:384], ACT.Copy).then_inc(mixedT_ready, 1)

            def squares(n, hp):
                act.wait_ge(pv_done, n + 1)
                for t in range(TB):
                    act.activation(o_norm[:, hp, t, :], ps[:, 5 + hp, t * SEQ:(t + 1) * SEQ], ACT.Square,
                                   accum_out=sq_sum[:, hp, t:t + 1]).then_inc(sq_done, 1)

            def o_hi_head(n, hp):
                act.wait_ge(o_turned, n + 1)
                act.activation(F[:, bass.ds(2 * n, 2), 0, :],
                               ps[:, 7 - 2 * hp, :].rearrange("p (e t) -> p e t", e=2), ACT.Copy).then_inc(o_hi, 1)

            def copy_v(k, bank_done, dst):
                act.wait_ge(*bank_done)
                act.activation(dst, ps[:, 4 * k, :], ACT.Copy).then_inc(v_copied, 1)

            def v_window(g, c):
                exps(2 * c, 0)
                copy_v(0, (first_block_done, c + 1), v_rows[:, 0, :])
                split_hi(g + 1, 0)
                exps(2 * c + 1, 1)
                copy_mixedT(2 * c, 0)
                split_hi(g + 1, 1)
                copy_v(1, (w_used, 4 * g + 4), v_rows[:, 1, :])
                split_hi(g + 1, 2)
                split_hi(g + 1, 3)

            split_some(1, 3)
            copy_halves(0, 0, 0, qk_half, 1, Q_SCALE)
            act.wait_ge(small_loaded, 64)
            act.activation(wz_hi[:, :, :], wz_raw, ACT.Copy).then_inc(wz_hi_ready, 1)
            act.wait_ge(lam_dots, 2)
            act.activation(lam_parts[:, 2:4], lam_parts[:, 0:2], ACT.Exp).then_inc(lam_exps, 1)
            split_hi(1, 3)
            split_some(2, 3)
            copy_halves(1, 1, 1, qk_half, 1)
            split_hi(2, 3)
            with act.Fori(0, PAIRS - 1) as c:
                v_window(3 * c + 2, c)
                g = 3 * c + 3
                split_hi(g + 1, 0)
                copy_mixedT(2 * c + 1, 1)
                squares(2 * c, 0)
                split_hi(g + 1, 1)
                squares(2 * c + 1, 1)
                split_hi(g + 1, 2)
                o_hi_head(2 * c, 0)
                o_hi_head(2 * c + 1, 1)
                copy_halves(g, 2 * c + 2, 0, qk_half, 1, Q_SCALE)
                split_hi(g + 1, 3)
                split_some(g + 2, 3)
                copy_halves(g + 1, 2 * c + 3, 1, qk_half, 1)
                split_hi(g + 2, 3)
            c = PAIRS - 1
            v_window(3 * c + 2, c)
            copy_mixedT(2 * c + 1, 1)
            squares(2 * c, 0)
            squares(2 * c + 1, 1)
            o_hi_head(2 * c, 0)
            split_hi(G_WO + 1, 0)
            o_hi_head(2 * c + 1, 1)
            for j in range(1, TILES):
                split_hi(G_WO + 1, j)
            with act.Fori(0, 2) as q:
                split_all(q + (G_WO + 2))

            def ln_window(g, L):
                if L == 4:
                    return
                split_hi(g + 1, 0)
                split_hi(g + 1, 1)
                x_hi_quarter(L, 0)
                x_hi_quarter(L, 1)
                split_hi(g + 1, 2)
                x_hi_quarter(L, 2)
                x_hi_quarter(L, 3)
                split_hi(g + 1, 3)
                for i in range(QUARTERS, TB * QUARTERS):
                    x_hi_quarter(L, i)

            ln_window(G_WO + 3, 1)

            def up_window(g, n, par, k, fk):
                split_some(g + 1, 3)
                copy_halves(g, n, par, mlp_half)
                split_hi(g + 1, 3)
                for s in range(2):
                    act.wait_ge(squared, k + (s + 1))
                    act.activation(F[:, bass.ds(fk + 2 * s, 2), 0, :], mlp_hidden[:, s], ACT.Copy).then_inc(f_hi, 1)

            def mlp(m, L):
                g0, n0 = G_MLP[m], COLS_MLP[m]
                with act.Fori(0, CHUNKS - 1) as ch:
                    with act.Fori(0, 2) as p:
                        for e in range(2):
                            up_window(8 * ch + 2 * p + (g0 + e), 4 * ch + 2 * p + (n0 + e), e,
                                      8 * ch + 4 * p + (32 * m + 2 * e), 8 * p + 4 * e)
                    with act.Fori(0, 4) as q:
                        split_all(8 * ch + q + (g0 + 5))
                ch = CHUNKS - 1
                with act.Fori(0, 2) as p:
                    for e in range(2):
                        up_window(2 * p + (g0 + e + 8 * ch), 2 * p + (n0 + e + 4 * ch), e,
                                  4 * p + (32 * m + 2 * e + 8 * ch), 8 * p + 4 * e)
                with act.Fori(0, 3) as q:
                    split_all(q + (g0 + 8 * ch + 5))
                ln_window(g0 + 8 * ch + 7, L + 1)

            mlp(0, 1)

            split_hi(G_GLA + 1, 0)
            split_hi(G_GLA + 1, 1)
            act.wait_ge(z_done, 1)
            act.activation(z_half[0:RANK, :], ps[0:RANK, 4, SEQ:], ACT.Copy).then_inc(z_half_copied, 1)
            split_hi(G_GLA + 1, 2)
            act.wait_ge(gk_done, 1)
            for i in range(KEY // P):
                a = act.activation(gate[:, i, :], ps[:, 4 + i // 2, (i % 2) * SEQ:(i % 2 + 1) * SEQ],
                                   ACT.Identity, bias=b_gk[:, i:i + 1])
            a.then_inc(gk_act, 1)
            act.wait_ge(gk_act, 1)
            act.activation(gk_tmp, gate, ACT.Abs).then_inc(gk_act, 1)
            act.wait_ge(gk_act, 2)
            act.activation(gk_tmp, gk_tmp, ACT.Exp, scale=-1.0).then_inc(gk_act, 1)
            act.wait_ge(gk_act, 3)
            act.activation(gk_tmp, gk_tmp, ACT.Ln, bias=1.0).then_inc(gk_act, 1)
            split_hi(G_GLA + 1, 3)
            act.wait_ge(scanned, 8)
            Gf = G[:, :, :, :, :].rearrange("p h e k t -> p (h e) k t")
            act.activation(Gf[:, :, G_QD, :], cum, ACT.Exp, scale=1.0 / TAU).then_inc(decays_ready, 1)
            copy_halves(G_GLA, COLS_GLA, 0, gla_half)
            split_some(G_GLA + 2, 3)
            act.activation(Gf[:, :, G_KI, :], cum, ACT.Exp, scale=-1.0 / TAU).then_inc(decays_ready, 1)
            act.wait_ge(to_last_ready, 1)
            act.activation(Gf[:, :, G_D, :].rearrange("p i (b c t) -> p i b c t", b=2, c=2)[:, :, :, 0, :],
                           to_last[:, :, 0::2, :], ACT.Exp, scale=1.0 / TAU).then_inc(decays_ready, 1)
            act.activation(Gf[:, :, G_R, CHUNK:P], to_last[:, :, 1, :], ACT.Exp, scale=1.0 / TAU
                           ).then_inc(decays_ready, 1)
            act.activation(chunk_decay[:, :, :],
                           cum.rearrange("p i (c t) -> p i c t", t=CHUNK)[:, :, 1:3, CHUNK - 1],
                           ACT.Exp, scale=1.0 / TAU).then_inc(decays_ready, 1)
            for u in range(1, 4):
                if u > 1:
                    split_some(G_GLA + 1 + u, 3)
                copy_halves(G_GLA + u, COLS_GLA + u, u % 2, gla_half)
                split_hi(G_GLA + 1 + u, 3)

            def o_hi_gla(h, t):
                act.wait_ge(go_turned, 2 * h + t + 1)
                act.activation(F[:, bass.ds(4 * h, 4), 0, blk(t)],
                               ps[:, 5 + t, :].rearrange("p (e t) -> p e t", t=P), ACT.Copy).then_inc(go_hi, 1)

            def exp_r_block(h, t):
                act.wait_ge(*((first_block_done, 2 * h + (ROWS_VR + 2)) if t == 0
                              else (w_used, 8 * h + 4 * (G_VR + 2))))
                if t:
                    act.wait_ge(r_gated, 2 * h + t)
                act.activation(sig, ps[:, 4 * t, :], ACT.Exp, scale=-1.0).then_inc(exp_r, 1)

            def r_window(h, last=False):
                act.wait_ge(pairs_done, h + 1)
                act.activation(pairT, ps[:, 1, 0:384], ACT.Copy).then_inc(pairs_copied, 1)
                exp_r_block(h, 0)
                split_hi(2 * h + (G_VR + 2), 0)
                act.wait_ge(go_done, h + 1)
                for t in range(TB):
                    act.activation(gla_o[:, t, :], ps[:, 2 + t, :], ACT.Square,
                                   accum_out=sq_sum[:, 0, t:t + 1]).then_inc(gsq_done, 1)
                split_hi(2 * h + (G_VR + 2), 1)
                split_hi(2 * h + (G_VR + 2), 2)
                if last:
                    exp_r_block(h, 1)
                split_hi(2 * h + (G_VR + 2), 3)
                if not last:
                    exp_r_block(h, 1)

            act.wait_ge(key_step, 8 * GLA_HEADS)
            copy_v(0, (first_block_done, ROWS_VR + 1), gla_v[:, 0, :])
            split_all(G_VR + 1)
            copy_v(1, (w_used, 4 * G_VR + 4), gla_v[:, 1, :])
            with act.Fori(0, GLA_HEADS - 1) as h:
                r_window(h)
                o_hi_gla(h, 0)
                o_hi_gla(h, 1)
                copy_v(0, (first_block_done, 2 * h + (ROWS_VR + 3)), gla_v[:, 0, :])
                split_all(2 * h + (G_VR + 3))
                copy_v(1, (w_used, 8 * h + 4 * (G_VR + 3)), gla_v[:, 1, :])
            h = GLA_HEADS - 1
            r_window(h, True)
            o_hi_gla(h, 0)
            o_hi_gla(h, 1)
            split_all(G_GWO + 1)
            with act.Fori(0, 2) as q:
                split_all(q + (G_GWO + 2))
            ln_window(G_GWO + 3, 3)
            mlp(1, 3)

        @block.vector
        def _(dve):
            def split_lo(g, j):
                dve.wait_ge(hi_ready, 4 * g + j + 1)
                dve.tensor_tensor(lo[:, j], raw[:, j], hi[:, j].bitcast(F32), ALU.subtract).then_inc(lo_ready, 1)

            def split_some(g, n):
                for j in range(n):
                    split_lo(g, j)

            def split_all(g):
                split_some(g, TILES)

            def x_lo_quarter(L, i):
                t, q = place(L, i)
                dve.wait_ge(x_hi, 8 * L + i + 1)
                dve.tensor_tensor(X[:, 4 * q:4 * q + 4, 1, blk(t)],
                                  ps[:, LN_BANKS[i % 3], :].rearrange("p (b t) -> p b t", t=P),
                                  X[:, 4 * q:4 * q + 4, 0, blk(t)].bitcast(F32), ALU.subtract).then_inc(x_lo, 1)

            def add_residual(t, col, done):
                dve.wait_ge(*done)
                d = res[:, t, bass.ds(col, COLS)]
                dve.tensor_tensor(d, d, ps[:, 4 * t, :], ALU.add).then_inc(res_added, 1)

            for i in range(TB * QUARTERS):
                x_lo_quarter(0, i)
                if i % 2:
                    split_lo(0, i // 2)

            def softmax_max(n, hp):
                if hp:
                    dve.wait_ge(mixed_ready, n)
                dve.wait_ge(scores_done, n + 1)
                dve.sem_inc(scores_seen, 1)
                for s in range(2):
                    for t, (a, b) in enumerate(((0, P), (P, 384))):
                        i = 2 * s + t
                        dve.tensor_tensor_reduce(probs[:, s, a:b], ps[:, 1 + s, a:b], mask[:, a:b], 1.0, MASKED,
                                                 ALU.add, ALU.max, row_max[:, i:i + 1]).then_inc(maxes, 1)
                dve.wait_ge(maxes, 4 * n + 4)
                dve.tensor_scalar(neg_max[:, :], row_max[:, :], -1.0, None, ALU.mult).then_inc(neg_max_ready, 1)

            def mix_maps(n, hp):
                dve.wait_ge(exps_done, 4 * n + 4)
                dve.reciprocal(inv_sum[:, :], row_sum[:, :]).then_inc(mix, 1)
                dve.wait_ge(mix, 4 * n + 1)
                dve.tensor_scalar(neg_lam_inv[:, :], inv_sum[:, 2:4], neg_lam[:, 0:1], None, ALU.mult).then_inc(mix, 1)
                dve.wait_ge(mix, 4 * n + 2)
                for t, (a, b) in enumerate(((0, P), (P, 384))):
                    dve.tensor_scalar(probs[:, 1, a:b], probs[:, 1, a:b], neg_lam_inv[:, t:t + 1], None,
                                      ALU.mult).then_inc(mix, 1)
                dve.wait_ge(mix, 4 * n + 4)
                if hp:
                    dve.wait_ge(mixed_turned, n)
                for t, (a, b) in enumerate(((0, P), (P, 384))):
                    m = dve.scalar_tensor_tensor(out=mixed[:, a:b], in0=probs[:, 0, a:b], scalar=inv_sum[:, t:t + 1],
                                                 in1=probs[:, 1, a:b], op0=ALU.mult, op1=ALU.add)
                m.then_inc(mixed_ready, 1)

            def normalise(n, hp):
                dve.wait_ge(sq_done, 2 * n + 2)
                dve.tensor_scalar(rms_rstd[:, hp, 0, :], sq_sum[:, hp, :], 1.0 / SEQ, RMS_EPS,
                                  ALU.mult, ALU.add).then_inc(ms_ready, 1)
                dve.wait_ge(rms_pow, n + 1)
                for t in range(TB):
                    dve.scalar_tensor_tensor(out=o_norm[:, hp, t, :], in0=ps[:, 5 + hp, t * SEQ:(t + 1) * SEQ],
                                             scalar=rms_rstd[:, hp, 1, t:t + 1], in1=subln,
                                             op0=ALU.mult, op1=ALU.mult).then_inc(o_normed, 1)

            def o_lo_head(n, hp):
                dve.wait_ge(o_hi, n + 1)
                dve.tensor_tensor(F[:, bass.ds(2 * n, 2), 1, :],
                                  ps[:, 7 - 2 * hp, :].rearrange("p (e t) -> p e t", e=2),
                                  F[:, bass.ds(2 * n, 2), 0, :].bitcast(F32), ALU.subtract).then_inc(o_lo, 1)

            def add_halves(n, par, dst, scale=None):
                for s in range(2):
                    dve.wait_ge(half_copied, 2 * n + (s + 1))
                    b = 4 * par + 2 * s
                    left = ps[:, b:b + 2, 0:SEQ]
                    if scale is None:
                        dve.tensor_tensor(dst[:, 2 * s:2 * s + 2, :], left, qk_half, ALU.add).then_inc(halves_added, 1)
                    else:
                        dve.scalar_tensor_tensor(out=dst[:, 2 * s:2 * s + 2, :], in0=left, scalar=scale, in1=qk_half,
                                                 op0=ALU.mult, op1=ALU.add).then_inc(halves_added, 1)

            def v_window(g, c):
                softmax_max(2 * c, 0)
                mix_maps(2 * c, 0)
                split_lo(g + 1, 0)
                softmax_max(2 * c + 1, 1)
                mix_maps(2 * c + 1, 1)
                split_lo(g + 1, 1)
                split_lo(g + 1, 2)
                split_lo(g + 1, 3)

            split_some(1, 3)
            add_halves(0, 0, qT, Q_SCALE)
            dve.wait_ge(consts_ready, 6)
            dve.wait_ge(small_loaded, 64)
            for i in range(2):
                dve.tensor_tensor_reduce(lam_rows[:, 2 * i, :], lam_rows[:, 2 * i, :], lam_rows[:, 2 * i + 1, :],
                                         1.0, 0.0, ALU.mult, ALU.add, lam_parts[:, i:i + 1]).then_inc(lam_dots, 1)
            dve.wait_ge(wz_hi_ready, 1)
            dve.tensor_tensor(wz_lo[:, :, :], wz_raw, wz_hi[:, :, :].bitcast(F32), ALU.subtract).then_inc(set_up, 1)
            dve.tensor_scalar(subln, subln, 1.0 - LAM_INIT, None, ALU.mult).then_inc(set_up, 1)
            dve.wait_ge(lam_exps, 1)
            dve.tensor_scalar(neg_lam[:, :], lam_parts[:, 3:4], lam_parts[:, 2:3], LAM_INIT,
                              ALU.subtract, ALU.subtract).then_inc(set_up, 1)
            split_lo(1, 3)
            split_some(2, 3)
            add_halves(1, 1, kT)
            split_lo(2, 3)
            with dve.Fori(0, PAIRS - 1) as c:
                v_window(3 * c + 2, c)
                g = 3 * c + 3
                split_lo(g + 1, 0)
                normalise(2 * c, 0)
                split_lo(g + 1, 1)
                normalise(2 * c + 1, 1)
                split_lo(g + 1, 2)
                o_lo_head(2 * c, 0)
                o_lo_head(2 * c + 1, 1)
                add_halves(2 * c + 2, 0, qT, Q_SCALE)
                split_lo(g + 1, 3)
                split_some(g + 2, 3)
                add_halves(2 * c + 3, 1, kT)
                split_lo(g + 2, 3)
            c = PAIRS - 1
            v_window(3 * c + 2, c)
            normalise(2 * c, 0)
            normalise(2 * c + 1, 1)
            o_lo_head(2 * c, 0)
            split_lo(G_WO + 1, 0)
            o_lo_head(2 * c + 1, 1)
            split_lo(G_WO + 1, 1)

            def stats_of(t, q, r, static):
                dve.wait_ge(res_added, 2 * r + (t + 1))
                if static:
                    dve.bn_stats(ln_stats[:, t, q, :], res[:, t, q * COLS:(q + 1) * COLS]).then_inc(ln_dve, 1)
                else:
                    dve.bn_stats(ln_stats[:, t, bass.ds(q, 1), :].rearrange("p a b -> p (a b)"),
                                 res[:, t, bass.ds(COLS * q, COLS)]).then_inc(ln_dve, 1)

            def out_window(g, q, r, rows, with_stats, static=False, late=False, split=0):
                if late:
                    for j in range(split, TILES - 1):
                        split_lo(g + 1, j)
                add_residual(0, COLS * q, (first_block_done, rows + 1))
                if with_stats:
                    stats_of(0, q, r, static)
                if late:
                    split_lo(g + 1, 3)
                else:
                    split_all(g + 1)
                add_residual(1, COLS * q, (w_used, 4 * g + 4))
                if with_stats:
                    stats_of(1, q, r, static)

            LN_STEPS = 2 * QUARTERS + TB * (1 + QUARTERS)

            def ln_start(L, t):
                at = ln_at(L, t)
                dve.wait_ge(ln_dve, at)
                dve.bn_aggr(ln_mean_var[:, t, :], ln_stats[:, t].rearrange("p a b -> p (a b)")).then_inc(ln_dve, 1)
                dve.wait_ge(ln_dve, at + 1)
                dve.tensor_scalar(ln_rstd[:, t, 0:1], ln_mean_var[:, t, 1:2], LN_EPS, None,
                                  ALU.add).then_inc(ln_var, 1)
                dve.wait_ge(gb_loaded, 32 * L)

            def centre(L, t, q):
                c = slice(q * COLS, (q + 1) * COLS)
                dve.scalar_tensor_tensor(out=res[:, t, c], in0=res[:, t, c], scalar=ln_mean_var[:, t, 0:1],
                                         in1=ln_gb[:, 0, c], op0=ALU.subtract, op1=ALU.mult).then_inc(ln_dve, 1)

            def scale(L, t, q):
                c = slice(q * COLS, (q + 1) * COLS)
                if q == 0:
                    dve.wait_ge(ln_pow, 2 * (L - 1) + t + 1)
                dve.wait_ge(ln_dve, ln_at(L, t) + 2 + q)
                dve.scalar_tensor_tensor(out=res[:, t, c], in0=res[:, t, c], scalar=ln_rstd[:, t, 1:2],
                                         in1=ln_gb[:, 1, c], op0=ALU.mult, op1=ALU.add).then_inc(ln_quarter, 1)

            def ln_at(L, t):
                return LN_STEPS * (L - 1) + (2 * QUARTERS - 1 + t) + t * (1 + QUARTERS)

            def ln_window(g, r, rows, L):
                q = QUARTERS - 1
                add_residual(0, COLS * q, (first_block_done, rows + 1))
                stats_of(0, q, r, True)
                ln_start(L, 0)
                for f, i in ((centre, 0), (centre, 1), (scale, 0), (centre, 2), (scale, 1), (centre, 3), (scale, 2),
                             (scale, 3)):
                    f(L, 0, i)
                if L < 4:
                    x_lo_quarter(L, 0)
                    x_lo_quarter(L, 1)
                    split_lo(g + 1, 0)
                    x_lo_quarter(L, 2)
                add_residual(1, COLS * q, (w_used, 4 * g + 4))
                stats_of(1, q, r, True)
                ln_start(L, 1)
                for i in range(QUARTERS):
                    centre(L, 1, i)
                    scale(L, 1, i)
                    if L < 4:
                        x_lo_quarter(L, 3 + i)
                        if i > 1:
                            split_lo(g + 1, i - 1)
                if L < 4:
                    x_lo_quarter(L, 7)
                    split_lo(g + 1, 3)

            dve.wait_ge(res_scaled, 8)
            out_window(G_WO, 0, 0, ROWS_WO, True, True, True, 2)
            with dve.Fori(1, QUARTERS - 1) as q:
                out_window(q + G_WO, q, q, q + ROWS_WO, True)
            ln_window(G_WO + 3, 3, ROWS_WO + 3, 1)

            def up_window(g, n, par, k, fk):
                split_some(g + 1, 3)
                dve.wait_ge(lo_ready, 4 * g + 7)
                for s in range(2):
                    dve.wait_ge(half_copied, 2 * n + (s + 1))
                    b = 4 * par + 2 * s
                    dve.tensor_tensor(mlp_hidden[:, s], ps[:, b:b + 2, 0:SEQ], mlp_half[:, s], ALU.add
                                      ).then_inc(halves_added, 1)
                for s in range(2):
                    dve.wait_ge(halves_added, 2 * n + (s + 1))
                    dve.scalar_tensor_tensor(out=mlp_hidden[:, s], in0=mlp_hidden[:, s], scalar=0.0,
                                             in1=mlp_hidden[:, s], op0=ALU.max, op1=ALU.mult).then_inc(squared, 1)
                split_lo(g + 1, 3)
                for s in range(2):
                    dve.wait_ge(f_hi, k + (s + 1))
                    dve.tensor_tensor(F[:, bass.ds(fk + 2 * s, 2), 1, :], mlp_hidden[:, s],
                                      F[:, bass.ds(fk + 2 * s, 2), 0, :].bitcast(F32), ALU.subtract
                                      ).then_inc(f_lo, 1)

            def mlp(m, L):
                g0, n0, r0, w0 = G_MLP[m], COLS_MLP[m], RES_MLP[m], ROWS_MLP[m]
                with dve.Fori(0, CHUNKS - 1) as ch:
                    with dve.Fori(0, 2) as p:
                        for e in range(2):
                            up_window(8 * ch + 2 * p + (g0 + e), 4 * ch + 2 * p + (n0 + e), e,
                                      8 * ch + 4 * p + (32 * m + 2 * e), 8 * p + 4 * e)
                    dve.wait_ge(res_scaled, 8 * (L + 1))
                    out_window(8 * ch + (g0 + 4), 0, 4 * ch + r0, 4 * ch + w0, False, True, True)
                    with dve.Fori(1, QUARTERS) as q:
                        out_window(8 * ch + q + (g0 + 4), q, 4 * ch + q + r0, 4 * ch + q + w0, False)
                ch = CHUNKS - 1
                with dve.Fori(0, 2) as p:
                    for e in range(2):
                        up_window(2 * p + (g0 + e + 8 * ch), 2 * p + (n0 + e + 4 * ch), e,
                                  4 * p + (32 * m + 2 * e + 8 * ch), 8 * p + 4 * e)
                out_window(g0 + 8 * ch + 4, 0, r0 + 4 * ch, w0 + 4 * ch, True, True, True)
                with dve.Fori(1, QUARTERS - 1) as q:
                    out_window(q + (g0 + 8 * ch + 4), q, q + (r0 + 4 * ch), q + (w0 + 4 * ch), True)
                ln_window(g0 + 8 * ch + 7, r0 + 4 * ch + 3, w0 + 4 * ch + 3, L + 1)

            mlp(0, 1)

            split_lo(G_GLA + 1, 0)
            split_lo(G_GLA + 1, 1)
            dve.wait_ge(z_half_copied, 1)
            dve.tensor_tensor(zT[0:RANK, :], ps[0:RANK, 4, 0:SEQ], z_half[0:RANK, :], ALU.add).then_inc(zT_ready, 1)
            split_lo(G_GLA + 1, 2)
            dve.wait_ge(gk_act, 4)
            dve.scalar_tensor_tensor(out=gate, in0=gate, scalar=0.0, in1=gk_tmp, op0=ALU.min, op1=ALU.subtract
                                     ).then_inc(gate_ready, 1)
            dve.wait_ge(gate_ready, 1)
            dve.wait_ge(consts_ready, 8)
            for i in range(GLA_HEADS * DKT):
                dve.tensor_tensor_scan(cum[:, i, :], scan_mask, gate[:, i, :], 0.0, ALU.mult, ALU.add
                                       ).then_inc(scanned, 1)
            split_lo(G_GLA + 1, 3)
            dve.wait_ge(scanned, 8)
            cc = cum.rearrange("p i (c t) -> p i c t", t=CHUNK)
            dve.tensor_tensor(to_last, cc[:, :, 0:3, CHUNK - 1:CHUNK].to_broadcast([P, GLA_HEADS * DKT, 3, CHUNK]),
                              cc[:, :, 0:3, :], ALU.subtract).then_inc(to_last_ready, 1)

            def gla_q(u):
                n = COLS_GLA + u
                if u:
                    dve.wait_ge(q_ready, 2 * u)
                for s in range(2):
                    dve.wait_ge(half_copied, 2 * n + s + 1)
                    b = 4 * (u % 2) + 2 * s
                    dve.tensor_tensor(gla_qk[:, s], ps[:, b:b + 2, 0:SEQ], gla_half[:, s], ALU.add
                                      ).then_inc(halves_added, 1)
                dve.wait_ge(decays_ready, 1)
                for s in range(2):
                    dve.wait_ge(halves_added, 2 * n + s + 1)
                    qd = G[:, 2 * u + s, :, G_QD, :]
                    dve.scalar_tensor_tensor(out=qd, in0=gla_qk[:, s], scalar=GLA_Q_SCALE, in1=qd,
                                             op0=ALU.mult, op1=ALU.mult).then_inc(q_ready, 1)

            def gla_k_sums(u):
                n = COLS_GLA + 2 + u
                dve.wait_ge(q_ready, 4)
                if u:
                    dve.wait_ge(key_step, 16 * u)
                for s in range(2):
                    dve.wait_ge(half_copied, 2 * n + s + 1)
                    b = 4 * (u % 2) + 2 * s
                    dve.tensor_tensor(gla_qk[:, s], ps[:, b:b + 2, 0:SEQ], gla_half[:, s], ALU.add
                                      ).then_inc(halves_added, 1)

            def gla_k(u):
                n = COLS_GLA + 2 + u
                dve.wait_ge(decays_ready, 5)
                for s in range(2):
                    h = 2 * u + s
                    step = 8 * h
                    dve.wait_ge(halves_added, 2 * n + s + 1)
                    k = gla_qk[:, s]
                    k4 = k.rearrange("p e (b c t) -> p e b c t", b=2, c=2)
                    inv = G[:, h, :, G_KI, :]
                    inv4 = inv.rearrange("p e (b c t) -> p e b c t", b=2, c=2)
                    d4 = G[:, h, :, G_D, :].rearrange("p e (b c t) -> p e b c t", b=2, c=2)
                    r = G[:, h, :, G_R, :]
                    dve.tensor_tensor(inv, inv, k, ALU.mult).then_inc(key_step, 1)
                    dve.tensor_tensor(d4[:, :, :, 0, :], d4[:, :, :, 0, :], k4[:, :, :, 0, :], ALU.mult
                                      ).then_inc(key_step, 1)
                    dve.tensor_tensor(r[:, :, CHUNK:P], r[:, :, CHUNK:P], k[:, :, CHUNK:P], ALU.mult
                                      ).then_inc(key_step, 1)
                    dve.wait_ge(key_step, step + 3)
                    dve.tensor_copy(d4[:, :, :, 1, :], inv4[:, :, :, 1, :]).then_inc(key_step, 1)
                    for e in range(DKT):
                        dve.tensor_scalar(r[:, e, 0:CHUNK], G[:, h, e, G_D, 0:CHUNK],
                                          chunk_decay[:, 2 * h + e, 0:1], None, ALU.mult).then_inc(key_step, 1)
                    dve.wait_ge(key_step, step + 6)
                    for e in range(DKT):
                        dve.tensor_scalar(r[:, e, P:2 * P], r[:, e, 0:P],
                                          chunk_decay[:, 2 * h + e, 1:2], None, ALU.mult).then_inc(key_step, 1)

            gla_q(0)
            split_some(G_GLA + 2, 3)
            gla_q(1)
            split_lo(G_GLA + 2, 3)
            split_some(G_GLA + 3, 3)
            gla_k_sums(0)
            split_lo(G_GLA + 3, 3)
            gla_k(0)
            split_some(G_GLA + 4, 3)
            gla_k_sums(1)
            split_lo(G_GLA + 4, 3)
            gla_k(1)
            split_all(G_VR + 1)

            def gate_r_block(h, t):
                dve.wait_ge(exp_r, 2 * h + (t + 1))
                dve.tensor_scalar(sig, sig, 1.0, None, ALU.add).then_inc(sig_step, 1)
                dve.wait_ge(sig_step, 4 * h + (2 * t + 1))
                dve.reciprocal(sig, sig).then_inc(sig_step, 1)
                dve.wait_ge(sig_step, 4 * h + (2 * t + 2))
                dve.tensor_tensor(silu_r[:, t, :], ps[:, 4 * t, :], sig, ALU.mult).then_inc(r_gated, 1)

            def norm_gla(h, t):
                dve.wait_ge(r_gained, 2 * h + (t + 1))
                dve.scalar_tensor_tensor(out=gla_o[:, t, :], in0=ps[:, 2 + t, :], scalar=rms_rstd[:, 0, 1, t:t + 1],
                                         in1=silu_r[:, t, :], op0=ALU.mult, op1=ALU.mult).then_inc(go_normed, 1)

            def r_window(h, last=False):
                gate_r_block(h, 0)
                split_lo(2 * h + (G_VR + 2), 0)
                dve.wait_ge(gsq_done, 2 * h + 2)
                dve.tensor_scalar(rms_rstd[:, 0, 0, :], sq_sum[:, 0, :], 1.0 / DV, RMS_EPS,
                                  ALU.mult, ALU.add).then_inc(gms_ready, 1)
                split_lo(2 * h + (G_VR + 2), 1)
                split_lo(2 * h + (G_VR + 2), 2)
                if not last:
                    split_lo(2 * h + (G_VR + 2), 3)
                gate_r_block(h, 1)
                dve.wait_ge(grms_pow, h + 1)
                norm_gla(h, 0)
                if last:
                    split_lo(2 * h + (G_VR + 2), 3)
                norm_gla(h, 1)

            def o_lo_gla(h, t):
                dve.wait_ge(go_hi, 2 * h + (t + 1))
                dve.tensor_tensor(F[:, bass.ds(4 * h, 4), 1, blk(t)],
                                  ps[:, 5 + t, :].rearrange("p (e t) -> p e t", t=P),
                                  F[:, bass.ds(4 * h, 4), 0, blk(t)].bitcast(F32), ALU.subtract).then_inc(go_lo, 1)

            with dve.Fori(0, GLA_HEADS - 1) as h:
                r_window(h)
                o_lo_gla(h, 0)
                o_lo_gla(h, 1)
                split_all(2 * h + (G_VR + 3))
            h = GLA_HEADS - 1
            r_window(h, True)
            o_lo_gla(h, 0)
            o_lo_gla(h, 1)
            dve.wait_ge(res_scaled, 24)
            out_window(G_GWO, 0, RES_GWO, ROWS_GWO, True, True, True)
            with dve.Fori(1, QUARTERS - 1) as q:
                out_window(q + G_GWO, q, q + RES_GWO, q + ROWS_GWO, True)
            ln_window(G_GWO + 3, RES_GWO + 3, ROWS_GWO + 3, 3)
            mlp(1, 3)


_INS = ["x", "attn_w_qkv", "attn_w_o", "attn_lambda", "attn_subln", "gla_w_in", "gla_w_gk2", "gla_b_gk",
        "gla_norm", "gla_w_o", "mlp_w1", "mlp_w2", "ln_g", "ln_b"]
_OUTS = [((1, SEQ, D), "float32")]


def kernel(**inputs):
    import numpy as _np
    import concourse.bacc as _bacc
    from concourse import mybir as _mybir
    from concourse.bass_utils import run_bass_kernel_spmd as _run

    nc = _bacc.Bacc("TRN2", target_bir_lowering=False, num_devices=1)
    arrays, args = {}, []
    for name in _INS:
        a = _np.ascontiguousarray(inputs[name])
        arrays[f"in_{name}_dram"] = a
        args.append(nc.dram_tensor(f"in_{name}_dram", a.shape, _mybir.dt.from_np(a.dtype), kind="ExternalInput").ap())
    for i, (shape, dtype) in enumerate(_OUTS):
        dt = _mybir.dt.from_np(_np.dtype(dtype))
        args.append(nc.dram_tensor(f"out_{i}_dram", shape, dt, kind="ExternalOutput").ap())
    build(nc, *args)
    r = _run(nc, [arrays], core_ids=[0])
    got = tuple(r.results[0][f"out_{i}_dram"] for i in range(len(_OUTS)))
    return got[0]
```
